# Optimizing a Trainium2 kernel written in Bass

```python
import math
import jax, jax.numpy as jnp
from jax import lax
import numpy as np

D_MODEL = 1024
BATCH = 1
SEQ = 1024
DEPTH = 1

POOL_WINDOWS = (2, 4, 8, 16)
POOL_GROUP = D_MODEL // 8
POOL_WIDTH = POOL_GROUP * len(POOL_WINDOWS)
N_HEADS = 8
HEAD_DIM = 64
ATTN_WIDTH = N_HEADS * HEAD_DIM
KV_LATENT = 128
IDX_HEADS = 8
IDX_DIM = 64
TOPK_MAX = 256
Q_BLOCK = 128
D_FF = 4 * D_MODEL
NUM_BUCKETS = 32
MAX_DISTANCE = 128
MAX_EXACT = NUM_BUCKETS // 2
ALPHA = (2 * DEPTH) ** 0.25
BETA = (8 * DEPTH) ** -0.25
LN_EPS = 1e-5

MIX_WIDTH = POOL_WIDTH + ATTN_WIDTH
SPLIT_SIZES = (POOL_WIDTH, ATTN_WIDTH, KV_LATENT, IDX_HEADS * IDX_DIM, IDX_DIM, IDX_HEADS)
D_IN = sum(SPLIT_SIZES)
SPLIT_POINTS = tuple(int(v) for v in np.cumsum(SPLIT_SIZES)[:-1])

kernel_name = "hymba_pool_dsa_deepnorm_trunk"

def layer_norm(x, g, b):
    xf = x.astype(jnp.float32)
    mu = jnp.mean(xf, axis=-1, keepdims=True)
    var = jnp.mean(jnp.square(xf - mu), axis=-1, keepdims=True)
    return ((xf - mu) * lax.rsqrt(var + LN_EPS) * g + b).astype(x.dtype)

def rms_norm(x, g):
    xf = x.astype(jnp.float32)
    return (xf * lax.rsqrt(jnp.mean(jnp.square(xf), axis=-1, keepdims=True) + LN_EPS) * g).astype(x.dtype)

def t5_causal_bucket(n):
    nf = jnp.maximum(n, 1).astype(jnp.float32)
    large = MAX_EXACT + (jnp.log(nf / MAX_EXACT) / math.log(MAX_DISTANCE / MAX_EXACT)
                         * (NUM_BUCKETS - MAX_EXACT)).astype(jnp.int32)
    large = jnp.minimum(large, NUM_BUCKETS - 1)
    return jnp.where(n < MAX_EXACT, n, large)

def causal_multiscale_pool(u):
    B, S, _ = u.shape
    uf = u.astype(jnp.float32).reshape(B, S, len(POOL_WINDOWS), POOL_GROUP)
    cs = jnp.concatenate([jnp.zeros_like(uf[:, :1]), jnp.cumsum(uf, axis=1)], axis=1)
    hi = cs[:, 1:]
    t = jnp.arange(S)
    outs = []
    for g, w in enumerate(POOL_WINDOWS):
        lo = jnp.pad(cs[:, :S + 1 - w, g], ((0, 0), (w - 1, 0), (0, 0)))
        cnt = jnp.minimum(t + 1, w).astype(jnp.float32)[None, :, None]
        outs.append((hi[:, :, g] - lo) / cnt - uf[:, :, g])
    return jnp.stack(outs, axis=2).astype(u.dtype)

def dsa_sparse_attention(q_lat, latent, iq, ik, iw, rel_bias):
    B, S = latent.shape[:2]
    k_sel = min(TOPK_MAX, S // 4)
    nb = S // Q_BLOCK
    key_pos = jnp.arange(S)

    def to_blocks(a):
        return jnp.moveaxis(a.reshape(B, nb, Q_BLOCK, *a.shape[2:]), 1, 0)

    def one_block(args):
        blk, qb, iqb, iwb = args
        q_pos = blk * Q_BLOCK + jnp.arange(Q_BLOCK)
        dots = jnp.einsum('bqhd,bsd->bqhs', iqb, ik).astype(jnp.float32) * IDX_DIM ** -0.5
        score = jnp.einsum('bqh,bqhs->bqs', iwb.astype(jnp.float32), jax.nn.relu(dots))
        causal = key_pos[None, :] <= q_pos[:, None]
        score = jnp.where(causal[None], score, -jnp.inf)
        _, idx = lax.top_k(score, k_sel)
        valid = idx <= q_pos[None, :, None]
        c_sel = jax.vmap(lambda c, i: c[i])(latent, idx)
        logits = jnp.einsum('bqhc,bqkc->bqhk', qb, c_sel).astype(jnp.float32) * HEAD_DIM ** -0.5
        bucket = t5_causal_bucket(jnp.maximum(q_pos[None, :, None] - idx, 0))
        bias = jnp.moveaxis(rel_bias[bucket].astype(jnp.float32), -1, 2)
        logits = jnp.where(valid[:, :, None, :], logits + bias, -jnp.inf)
        p = jax.nn.softmax(logits, axis=-1).astype(c_sel.dtype)
        return jnp.einsum('bqhk,bqkc->bqhc', p, c_sel)

    out = lax.map(one_block, (jnp.arange(nb), to_blocks(q_lat), to_blocks(iq), to_blocks(iw)))
    return jnp.moveaxis(out, 0, 1).reshape(B, S, N_HEADS, KV_LATENT)

def setup_inputs(seed: int = 0) -> dict:
    key = jax.random.key(seed)
    ks = jax.random.split(key, 20)

    def nrm(k, shape, scale):
        return jax.random.normal(k, shape, jnp.float32) * scale

    L = DEPTH
    return {
        "x": nrm(ks[0], (BATCH, SEQ, D_MODEL), 1.0),
        "emb_ln_g": 1.0 + nrm(ks[1], (D_MODEL,), 0.02),
        "emb_ln_b": nrm(ks[2], (D_MODEL,), 0.02),
        "rel_bias": nrm(ks[3], (NUM_BUCKETS, N_HEADS), 0.5),
        "w_in": nrm(ks[4], (L, D_MODEL, D_IN), D_MODEL ** -0.5),
        "pool_w": nrm(ks[5], (L, len(POOL_WINDOWS), POOL_GROUP, POOL_GROUP), POOL_GROUP ** -0.5),
        "pool_scale": 1.0 + nrm(ks[6], (L, POOL_WIDTH), 0.02),
        "kv_norm_g": 1.0 + nrm(ks[7], (L, KV_LATENT), 0.02),
        "w_uk": nrm(ks[8], (L, KV_LATENT, N_HEADS, HEAD_DIM), KV_LATENT ** -0.5),
        "w_uv": nrm(ks[9], (L, KV_LATENT, N_HEADS, HEAD_DIM), KV_LATENT ** -0.5 * BETA),
        "w_o": nrm(ks[10], (L, MIX_WIDTH, D_MODEL), MIX_WIDTH ** -0.5 * BETA),
        "ln1_g": 1.0 + nrm(ks[11], (L, D_MODEL), 0.02),
        "ln1_b": nrm(ks[12], (L, D_MODEL), 0.02),
        "w_up": nrm(ks[13], (L, D_MODEL, D_FF), D_MODEL ** -0.5),
        "w_down": nrm(ks[14], (L, D_FF, D_MODEL), D_FF ** -0.5 * BETA),
        "ln2_g": 1.0 + nrm(ks[15], (L, D_MODEL), 0.02),
        "ln2_b": nrm(ks[16], (L, D_MODEL), 0.02),
    }

def reference(x, emb_ln_g, emb_ln_b, rel_bias, w_in, pool_w, pool_scale, kv_norm_g,
              w_uk, w_uv, w_o, ln1_g, ln1_b, w_up, w_down, ln2_g, ln2_b):
    B, S, _ = x.shape
    x = layer_norm(x, emb_ln_g, emb_ln_b)
    for l in range(DEPTH):
        proj = x @ w_in[l]
        u_pool, q, c, iq, ik, iw = jnp.split(proj, SPLIT_POINTS, axis=-1)
        pooled = causal_multiscale_pool(u_pool)
        pool_out = jnp.einsum('bsgc,gcd->bsgd', pooled, pool_w[l]).reshape(B, S, POOL_WIDTH) * pool_scale[l]
        q = q.reshape(B, S, N_HEADS, HEAD_DIM)
        q_lat = jnp.einsum('bshd,chd->bshc', q, w_uk[l])
        c = rms_norm(c, kv_norm_g[l])
        iq = iq.reshape(B, S, IDX_HEADS, IDX_DIM)
        iw = iw * IDX_HEADS ** -0.5
        o_lat = dsa_sparse_attention(q_lat, c, iq, ik, iw, rel_bias)
        attn_out = jnp.einsum('bshc,chd->bshd', o_lat, w_uv[l]).reshape(B, S, ATTN_WIDTH)
        mix = jnp.concatenate([pool_out, attn_out], axis=-1) @ w_o[l]
        x = layer_norm(ALPHA * x + mix, ln1_g[l], ln1_b[l])
        ff = jnp.square(jax.nn.relu(x @ w_up[l])) @ w_down[l]
        x = layer_norm(ALPHA * x + ff, ln2_g[l], ln2_b[l])
    return x


_drawn_inputs = setup_inputs


def setup_inputs(seed=0):
    import zlib

    import numpy as np

    out = dict(_drawn_inputs(seed))
    spreads = {}
    factors = {'emb_ln_b': 2.691,
     'rel_bias': 6.246,
     'pool_scale': 8.0,
     'kv_norm_g': 8.0,
     'ln1_g': 2.713,
     'ln1_b': 2.799,
     'ln2_g': 2.853,
     'ln2_b': 2.857}
    for name, (base, spread) in spreads.items():
        noise = np.random.default_rng([zlib.crc32(name.encode()), seed]).standard_normal(out[name].shape)
        drawn = base * np.exp(spread * noise) if base else spread * noise
        out[name] = __import__('jax').numpy.asarray(drawn.astype(out[name].dtype))
    for name, factor in factors.items():
        out[name] = (out[name] * factor).astype(out[name].dtype)
    return out
```

```python
from contextlib import ExitStack

import numpy as np

import concourse.bass as bass
from concourse import mybir

F32 = mybir.dt.float32
ALU = mybir.AluOpType
ACT = mybir.ActivationFunctionType

P = 128
S = 1024
D = 1024
KT = D // P
CHUNK = 512
CB = CHUNK // P
NB = S // P
HEADS = 8
HD = 64
LAT = 128
WINDOWS = (2, 4, 8, 16)
TOPK = 256
FF = 4 * D
NBUCKET = 32
MAX_DIST = 128
ALPHA = 2.0 ** 0.25
EPS = 1e-5
NEG = -1.0e30
TAKEN = -3.0e38
HIST = 16
NEAR = 2 * P
FWIN = NEAR + P

COL_U, COL_Q, COL_C, COL_IQ = 0, 512, 1024, 1152
COL_IK = COL_IQ + HEADS * HD
COL_IW = COL_IK + HD
ROWW = LAT + HEADS
GT = 8
GROUPS = FF // P // GT
GUSES = GT + 2 * CB


def bucket_differences():
    n = np.maximum(NEAR - 1 - np.arange(FWIN), 0)
    exact = NBUCKET // 2
    large = exact + (np.log(np.maximum(n, 1) / exact) / np.log(MAX_DIST / exact) * exact).astype(np.int64)
    bucket = np.where(n < exact, n, np.minimum(large, NBUCKET - 1))
    hot = (np.arange(NBUCKET)[:, None] == bucket[None, :]).astype(np.float32)
    hot[NBUCKET - 1] -= 1.0
    return hot


def psum_uses():
    names = ["vecs", "wuk", "bias"]

    def attention(c):
        out = []
        for step in range(32 * c, 32 * c + 32 + 5):
            out += attention_step(c, step)
        return out

    names += [("xT", 0, k) for k in range(KT)]
    names += [("row", b) for b in range(CB)] + [("cT", 0), ("ik", 0)] + [("iq", 0, p) for p in range(4)]
    names += [("xT", 1, k) for k in range(KT)] + [("near", n) for n in range(4)]
    names += branches(0)
    names += [("row", CB + b) for b in range(CB)] + [("cT", 1), ("ik", 1)] + [("iq", 1, p) for p in range(4)]
    names += attention(0) + [("x1T", 0, k) for k in range(KT)] + [("mlp", 0, n) for n in range(GROUPS * GUSES)]
    names += branches(1)
    names += attention(1) + [("x1T", 1, k) for k in range(KT)] + [("mlp", 1, n) for n in range(GROUPS * GUSES)]
    return {name: k for k, name in enumerate(names)}


def branches(c):
    out = []
    for p in range(4):
        out += [("q", c, p)]
        if p:
            out += [("ql", c, 2 * p - 2), ("ql", c, 2 * p - 1)]
    for g in range(4):
        out += [("u", c, g)]
        if g == 0:
            out += [("ql", c, 6), ("ql", c, 7)]
        if g >= 2:
            out += [("po", c, g - 2)]
    return out + [("po", c, 2), ("po", c, 3)]


def attention_step(c, step):
    lo, hi = 32 * c, 32 * c + 32
    out = []
    if step < hi:
        i = step // HEADS
        out += [("tr", step, t) for t in range((i + 4) // 4)]
    if step % 2 == 0 and lo <= step - 2 < hi:
        out += [("pv", (step - 2) // 2)]
    if step % 2 == 1 and lo <= step - 3 < hi:
        out += [("uv", (step - 3) // 2)]
    if step % HEADS == 4 and lo <= step - 12 < hi:
        out += [("aT", (step - 12) // HEADS)]
    return out


LAST_STEP = 32 + 5


def layer(nc, x, emb_ln_g, emb_ln_b, rel_bias, w_in, pool_w, pool_scale, kv_norm_g, w_uk, w_uv, w_o,
          ln1_g, ln1_b, w_up, w_down, ln2_g, ln2_b, buckets, spill, bias_rows, out):
    G = psum_uses()
    xd = x.rearrange("o (b p) d -> (o b) p d", p=P)
    outd = out.rearrange("o (b p) d -> (o b) p d", p=P)
    spilld = spill.rearrange("(b p) d -> b p d", p=P)
    wind = w_in.rearrange("o (k p) n -> p (o k) n", p=P)
    wod = w_o.rearrange("o (k p) n -> p (o k) n", p=P)
    wupd = w_up.rearrange("o (k p) n -> p (o k) n", p=P)
    wdownd = w_down.rearrange("o (f p) n -> p (o f) n", p=P)

    with ExitStack() as ctx:
        def sb(name, shape, dt=F32):
            return ctx.enter_context(nc.sbuf_tensor(name, shape, dt))

        def sem(name):
            return ctx.enter_context(nc.semaphore(name))

        g_bank = [ctx.enter_context(nc.psum_tensor(f"g_bank{i}", [P, 512], F32)) for i in range(4)]
        wide = [ctx.enter_context(nc.psum_tensor(f"wide{i}", [P, 1024], F32)) for i in range(2)]

        def bank(name):
            return g_bank[G[name] % 4]

        rows = sb("rows", [P, CB, D])
        xT = [sb(f"xT{c}", [P, KT, CHUNK]) for c in range(2)]
        wring = [sb(f"wring{s}", [P, D]) for s in range(4)]
        score = sb("score", [P, CB, S])
        work = sb("work", [P, S])
        near_bias = sb("near_bias", [P, HEADS, NEAR])
        iqT = sb("iqT", [P, 4, CHUNK])
        ikT = sb("ikT", [P, S])
        lat = sb("lat", [P, NB, LAT])
        latT = sb("latT", [P, S])
        gains = sb("gains", [P, 2, D])
        ident = sb("ident", [P, P])
        flip = sb("flip", [P, P])
        wukT = sb("wukT", [P, 4, LAT])
        wuv = sb("wuv", [P, HEADS * HD])
        poolw = sb("poolw", [P, 4, P])
        roww = sb("roww", [P, KT, ROWW])
        kvg = sb("kvg", [P, LAT])
        vec_rows = sb("vec_rows", [36, P])
        vecs = sb("vecs", [P, 36])
        relb = sb("relb", [NBUCKET, HEADS])
        bias_row = sb("bias_row", [HEADS, FWIN])
        recip_count = sb("recip_count", [P, HIST])
        count = sb("count", [P, HIST])
        hist = sb("hist", [P, 4, HIST])
        craw = sb("craw", [P, 2, LAT])
        csq = sb("csq", [P, LAT])
        idx_w = sb("idx_w", [P, NB, HEADS])
        stats = sb("stats", [P, CB, 12])
        mean_var = sb("mean_var", [P, 6 * CB, 2])
        rstd = sb("rstd", [P, 6 * CB])
        power = sb("power", [P, 1])
        csum = sb("csum", [P, NB])
        crstd = sb("crstd", [P, NB])
        top8 = sb("top8", [P, 8])
        row_max = sb("row_max", [P, 2])
        neg_max = sb("neg_max", [P, 2])
        exp_sum = sb("exp_sum", [P, 2, HEADS])
        exp_rec = sb("exp_rec", [P, 2, HEADS])
        oT = sb("oT", [P, 2, P])
        att = sb("att", [P, 2, 512])

        area1 = sb("area1", [P, 8 * D])
        area2 = sb("area2", [P, 4096])
        area3 = sb("area3", [P, 4096])
        xstage = area1[:, :].rearrange("p (b d) -> p b d", d=D)
        qlatT = area1[:, 0:4096].rearrange("p (h s) -> p h s", s=CHUNK)
        mixT = area1[:, 4096:8192].rearrange("p (k s) -> p k s", s=CHUNK)
        wdown_sb = area1[:, :].rearrange("p (f d) -> p f d", d=D)
        relu_sb = area2[:, 0:2048].rearrange("p (u s) -> p u s", u=2)
        wuk_raw = area2[:, 3072:3584]
        hots = area2[0:NBUCKET, 3584:3584 + FWIN]
        near_up = area2[:, 0:2048].rearrange("p (h n) -> p h n", h=HEADS)
        qT = area2[:, 2048:3072].rearrange("p (u s) -> p u s", u=2)
        probsT = area2[:, :].rearrange("p (u k h q) -> p u k h q", u=2, k=NB, h=2)
        hT = area2[:, :].rearrange("p (f s) -> p f s", f=GT)
        logit = area3[:, 0:2048].rearrange("p (u s) -> p u s", u=2)
        mask = area3[:, 2048:4096].rearrange("p (u s) -> p u s", u=2)
        uT = area3[:, 0:1056].rearrange("p (u s) -> p u s", u=2)
        win = area3[:, 1056:2112].rearrange("p (u s) -> p u s", u=2)
        pooledT = area3[:, 2112:3136].rearrange("p (u s) -> p u s", u=2)
        relu_h = area3[:, 0:1024].rearrange("p (u s) -> p u s", u=2)
        y_stage = area3[:, 1024:2048].rearrange("p (u s) -> p u s", u=2)

        emb_g, emb_b, l1_g, l1_b = (vecs[:, 8 * n:8 * n + 8] for n in range(4))
        pscale = vecs[:, 32:36]

        x_in = [sem(f"x_in{b}") for b in range(NB)]
        small_in = sem("small_in")
        late_in = sem("late_in")
        roww_in = sem("roww_in")
        ring_in = [sem(f"ring_in{s}") for s in range(4)]
        gains_in = sem("gains_in")
        wdown_in = sem("wdown_in")
        rows_in = sem("rows_in")
        spilled = sem("spilled")
        bias_out = sem("bias_out")
        bias_in = sem("bias_in")
        stored = sem("stored")
        g_full = sem("g_full")
        g_evac = sem("g_evac")
        bias_row_ready = sem("bias_row_ready")
        ident_ready = sem("ident_ready")
        const_steps = sem("const_steps")
        counts_ready = sem("counts_ready")
        masks01_ready = sem("masks01_ready")
        dve_steps = sem("dve_steps")
        stats_ready = sem("stats_ready")
        var_eps = sem("var_eps")
        rstd_ready = sem("rstd_ready")
        xhat_ready = sem("xhat_ready")
        gain_mul = sem("gain_mul")
        gained = sem("gained")
        craw_ready = sem("craw_ready")
        csum_ready = sem("csum_ready")
        lat_steps = sem("lat_steps")
        lat_ready = sem("lat_ready")
        dots_full = sem("dots_full")
        relu_ready = sem("relu_ready")
        score_added = sem("score_added")
        diag_masked = sem("diag_masked")
        topk_steps = sem("topk_steps")
        topk_turn = sem("topk_turn")
        mask_ready = sem("mask_ready")
        pool_steps = sem("pool_steps")
        pooled_ready = sem("pooled_ready")
        mask_full = sem("mask_full")
        logits_full = sem("logits_full")
        masked = sem("masked")
        neg_max_ready = sem("neg_max_ready")
        exp_ready = sem("exp_ready")
        att_ready = sem("att_ready")
        wo_used = sem("wo_used")
        wo_full = sem("wo_full")
        wo_added = sem("wo_added")
        h_ready = sem("h_ready")
        y_added = sem("y_added")

        units = []
        for c in range(2):
            if c == 0:
                units += [("ik", 0)] + [("iq", 0, p) for p in range(4)] + [("q", 0, p) for p in range(4)]
                units += [("u", 0, g) for g in range(4)] + [("ik", 1)] + [("iq", 1, p) for p in range(4)]
            else:
                units += [("q", 1, p) for p in range(4)] + [("u", 1, g) for g in range(4)]
            units += [("wo", c, nh, u) for nh in range(2) for u in range(4)]
            units += [("up", c, t) for t in range(GROUPS * GT)]
        U = {name: n for n, name in enumerate(units)}

        def unit_tile(name):
            return wring[U[name] % 4]

        def unit_arrived(eng, name):
            eng.wait_ge(ring_in[U[name] % 4], 16 * (U[name] // 4 + 1))

        LN = {("emb", 0): 0, ("emb", 1): 1, ("ln1", 0): 2, ("ln2", 0): 3, ("ln1", 1): 4, ("ln2", 1): 5}

        def gained_at(which, c, b):
            return 4 * LN[(which, c)] + b + 1

        block = ctx.enter_context(nc.Block())

        @block.sync
        def _(sp):
            sp.dma_start(vec_rows[0:8, :], emb_ln_g.rearrange("(k p) -> k p", p=P)).then_inc(small_in, 16)
            sp.dma_start(vec_rows[8:16, :], emb_ln_b.rearrange("(k p) -> k p", p=P)).then_inc(small_in, 16)
            sp.dma_start(vec_rows[16:24, :], ln1_g.rearrange("o (k p) -> (o k) p", p=P)).then_inc(small_in, 16)
            sp.dma_start(vec_rows[24:32, :], ln1_b.rearrange("o (k p) -> (o k) p", p=P)).then_inc(small_in, 16)
            sp.dma_start(vec_rows[32:36, :], pool_scale.rearrange("o (k p) -> (o k) p", p=P)).then_inc(small_in, 16)
            for b in range(2):
                sp.dma_start(xstage[:, b, :], xd[b]).then_inc(x_in[b], 16)
            sp.dma_start(wuk_raw[:, :], w_uk.rearrange("o c h d -> (o c) (h d)")).then_inc(small_in, 16)
            sp.dma_start(relb[:, :], rel_bias).then_inc(small_in, 16)
            sp.dma_start(hots[:, :], buckets).then_inc(small_in, 16)
            for b in range(2, CB):
                sp.dma_start(xstage[:, b, :], xd[b]).then_inc(x_in[b], 16)
            sp.dma_start(roww[:, :, 0:LAT], wind[:, :, COL_C:COL_C + LAT]).then_inc(roww_in, 16)
            with nc.allow_non_contiguous_dma(reason="eight indexer weight columns"):
                sp.dma_start(roww[:, :, LAT:ROWW], wind[:, :, COL_IW:COL_IW + HEADS]).then_inc(roww_in, 16)
            sp.dma_start(kvg[:, :], kv_norm_g.to_broadcast([P, LAT])).then_inc(roww_in, 16)

            def load_in(name):
                n = U[name]
                tile = unit_tile(name)[:, :].rearrange("p (k n) -> p k n", k=KT)
                if name[0] == "ik":
                    for half in range(2):
                        sp.dma_start(tile[:, :, half * HD:half * HD + HD],
                                     wind[:, :, COL_IK:COL_IK + HD]).then_inc(ring_in[n % 4], 16)
                    return
                col = {"iq": COL_IQ, "q": COL_Q, "u": COL_U}[name[0]] + P * name[2]
                sp.dma_start(tile, wind[:, :, col:col + P]).then_inc(ring_in[n % 4], 16)

            def slot_free(name):
                n = U[name] - 4
                if n < 0:
                    return
                old = units[n]
                if old[0] == "wo" and old[3] == 3:
                    sp.wait_ge(wo_full, 8 * old[1] + 4 * old[2] + 4)
                elif old[0] == "wo":
                    sp.wait_ge(wo_used, 6 * old[1] + 3 * old[2] + old[3] + 1)
                elif old[0] == "up":
                    sp.wait_ge(g_full, G[("mlp", old[1], old[2] // GT * GUSES + old[2] % GT)] + 1)
                else:
                    sp.wait_ge(g_full, G[old] + 1)

            def load_wo(c):
                for nh in range(2):
                    for u in range(4):
                        name = ("wo", c, nh, u)
                        slot_free(name)
                        sp.dma_start(unit_tile(name)[:, :].rearrange("p (k n) -> p k n", k=2),
                                     wod[:, 2 * u:2 * u + 2, nh * 512:nh * 512 + 512]).then_inc(ring_in[U[name] % 4], 16)

            def load_gains(g, b):
                sp.dma_start(gains[:, 0, :], g.to_broadcast([P, D])).then_inc(gains_in, 16)
                sp.dma_start(gains[:, 1, :], b.to_broadcast([P, D])).then_inc(gains_in, 16)

            def load_mlp(c):
                first = U[("up", c, 0)]
                base = G[("mlp", c, 0)]
                sp.wait_ge(wo_full, 8 * c + 8)

                def up(g, t):
                    slot = (first + t) % 4
                    col = g * (GT * P) + t * P
                    sp.dma_start(wring[slot][:, :].rearrange("p (k n) -> p k n", k=KT),
                                 wupd[:, :, bass.ds(col, P)]).then_inc(ring_in[slot], 16)

                with sp.Fori(0, GROUPS) as g:
                    for t in range(4):
                        sp.wait_ge(g_full, g * GUSES + (base - GUSES + t + 4 + 1))
                        up(g, t)
                    sp.wait_ge(g_full, g * GUSES + base)
                    sp.dma_start(wdown_sb, wdownd[:, bass.ds(g * GT, GT), :]).then_inc(wdown_in, 16)
                    for t in range(4, GT):
                        sp.wait_ge(g_full, g * GUSES + (base + t - 4 + 1))
                        up(g, t)

            def store(c):
                for b in range(CB):
                    sp.wait_ge(gained, gained_at("ln2", c, b))
                    sp.dma_start(outd[CB * c + b], rows[:, b, :]).then_inc(stored, 16)

            for n in range(4):
                load_in(units[n])
            for b in range(CB, NB):
                sp.dma_start(xstage[:, b, :], xd[b]).then_inc(x_in[b], 16)
            load_gains(emb_ln_g.rearrange("(o d) -> o d", o=1), emb_ln_b.rearrange("(o d) -> o d", o=1))
            sp.dma_start(wuv[:, :], w_uv.rearrange("o c h d -> (o c) (h d)")).then_inc(late_in, 16)
            sp.dma_start(poolw[:, :, :], pool_w.rearrange("o g c d -> c (o g) d")).then_inc(late_in, 16)
            sp.wait_ge(bias_row_ready, 1)
            sp.dma_start(bias_rows, bias_row[:, :]).then_inc(bias_out, 16)
            sp.wait_ge(bias_out, 16)
            sp.dma_start(near_up, bass.AP(tensor=bias_rows.tensor, offset=0, ap=[[1, P], [FWIN, HEADS], [1, NEAR]])
                         ).then_inc(bias_in, 16)
            for n in range(4, U[("wo", 0, 0, 0)]):
                slot_free(units[n])
                load_in(units[n])
                if n == 6:
                    for b in range(NB):
                        sp.wait_ge(gained, b + 1)
                        sp.dma_start(spilld[b], xstage[:, b, :]).then_inc(spilled, 16)
                    load_gains(ln1_g, ln1_b)
                    sp.wait_ge(spilled, 16 * NB)
                    for b in range(CB):
                        sp.dma_start(rows[:, b, :], spilld[b]).then_inc(rows_in, 16)
            load_wo(0)
            load_mlp(0)
            for p in range(4):
                slot_free(("q", 1, p))
                load_in(("q", 1, p))
            sp.wait_ge(gained, gained_at("ln1", 0, CB - 1))
            load_gains(ln2_g, ln2_b)
            store(0)
            load_gains(ln1_g, ln1_b)
            sp.wait_ge(stored, 16 * CB)
            for b in range(CB):
                sp.dma_start(rows[:, b, :], spilld[CB + b]).then_inc(rows_in, 16)
            for g in range(4):
                slot_free(("u", 1, g))
                load_in(("u", 1, g))
            load_wo(1)
            load_mlp(1)
            sp.wait_ge(gained, gained_at("ln1", 1, CB - 1))
            load_gains(ln2_g, ln2_b)
            store(1)
            sp.wait_ge(stored, 16 * NB)

        @block.gpsimd
        def _(pool):
            n_const = 0
            pool.memset(ident[:, :], 0.0).then_inc(const_steps, 1)
            pool.wait_ge(const_steps, 1)
            pool.affine_select(out=ident[:, :], in_=ident[:, :], compare_op=ALU.not_equal, fill=1.0, base=0,
                               pattern=[[-1, P]], channel_multiplier=1).then_inc(ident_ready, 1)
            pool.memset(flip[:, :], 0.0).then_inc(const_steps, 1)
            pool.wait_ge(const_steps, 2)
            pool.affine_select(out=flip[:, :], in_=flip[:, :], compare_op=ALU.not_equal, fill=1.0, base=1 - P,
                               pattern=[[1, P]], channel_multiplier=1).then_inc(ident_ready, 1)
            pool.memset(power[:, :], -0.5).then_inc(const_steps, 1)
            pool.memset(csum[:, :], 0.0).then_inc(y_added, 2)
            pool.iota(count[:, :], pattern=[[1, HIST]], base=1, channel_multiplier=0,
                      allow_small_or_imprecise_dtypes=True).then_inc(counts_ready, 1)
            pool.memset(hist[:, :, :], 0.0).then_inc(const_steps, 1)
            for i in range(2):
                pool.memset(score[:, i, 0:CHUNK], 0.0).then_inc(const_steps, 1)
            pool.wait_ge(const_steps, 6)
            for i in range(2):
                diag = score[:, i, i * P:(i + 1) * P]
                pool.affine_select(out=diag, in_=diag, compare_op=ALU.is_ge, fill=NEG, base=0,
                                   pattern=[[-1, P]], channel_multiplier=1).then_inc(masks01_ready, 1)

            def inverse_std(l):
                for b in range(CB):
                    n = 4 * l + b
                    pool.wait_ge(stats_ready, n + 1)
                    pool.tensor_scalar(rstd[:, n:n + 1], mean_var[:, n, 1:2], EPS, None, ALU.add).then_inc(var_eps, 1)
                    pool.wait_ge(var_eps, n + 1)
                    pool.tensor_tensor(rstd[:, n:n + 1], rstd[:, n:n + 1], power[:, :], ALU.pow).then_inc(rstd_ready, 1)

            def times_gain(which, c, tiles, loads, after):
                l = LN[(which, c)]
                for b in range(CB):
                    n = 4 * l + b
                    if b == 0:
                        pool.wait_ge(gains_in, 32 * loads)
                        after()
                    pool.wait_ge(xhat_ready, n + 1)
                    pool.tensor_tensor(tiles[:, b, :], tiles[:, b, :], gains[:, 0, :], ALU.mult).then_inc(pool_steps, 1)
                    mark()
                    last = pool.tensor_tensor(tiles[:, b, :], tiles[:, b, :], gains[:, 1, :], ALU.add)
                    if which == "ln1":
                        last.then_inc(pool_steps, 1)
                        mark()
                        last = pool.tensor_scalar(tiles[:, b, :], tiles[:, b, :], ALPHA, None, ALU.mult)
                    last.then_inc(gained, 1)

            steps = [0]

            def mark():
                steps[0] += 1
                pool.wait_ge(pool_steps, steps[0])

            def latents(c):
                if c == 0:
                    pool.wait_ge(roww_in, 48)
                for b in range(CB * c, CB * c + CB):
                    pool.wait_ge(csum_ready, b + 1)
                    pool.tensor_scalar(crstd[:, b:b + 1], csum[:, b:b + 1], 1.0 / LAT, EPS, ALU.mult, ALU.add)\
                        .then_inc(pool_steps, 1)
                    mark()
                    pool.tensor_tensor(crstd[:, b:b + 1], crstd[:, b:b + 1], power[:, :], ALU.pow).then_inc(pool_steps, 1)
                    mark()
                    pool.tensor_scalar(lat[:, b, :], craw[:, b % 2, :], crstd[:, b:b + 1], None, ALU.mult)\
                        .then_inc(pool_steps, 1)
                    mark()
                    pool.tensor_tensor(lat[:, b, :], lat[:, b, :], kvg[:, :], ALU.mult).then_inc(lat_ready, 1)

            def diagonals(blocks):
                for i in blocks:
                    pool.wait_ge(score_added, 8 * (i - 2) + 8)
                    diag = score[:, i % CB, i * P:(i + 1) * P]
                    pool.affine_select(out=diag, in_=diag, compare_op=ALU.is_ge, fill=TAKEN, base=0,
                                       pattern=[[-1, P]], channel_multiplier=1).then_inc(diag_masked, 1)

            def pooling(c):
                for g, w in enumerate(WINDOWS):
                    u = uT[:, g % 2, :]
                    pool.wait_ge(g_evac, G[("u", c, g)] + 1)
                    if c == 0 and g == 0:
                        pool.wait_ge(counts_ready, 2)
                    pool.tensor_copy(u[:, 0:HIST], hist[:, g, :]).then_inc(pool_steps, 1)
                    mark()
                    src, reach = u, 1
                    while reach < w:
                        dst = win[:, (reach.bit_length() - 1) % 2, :]
                        pool.tensor_tensor(dst[:, reach:HIST + CHUNK], src[:, reach:HIST + CHUNK],
                                           src[:, 0:HIST + CHUNK - reach], ALU.add).then_inc(pool_steps, 1)
                        mark()
                        src, low, reach = dst, reach, 2 * reach
                        if reach < w:
                            pool.tensor_copy(dst[:, 0:low], u[:, 0:low]).then_inc(pool_steps, 1)
                            mark()
                    done = pooledT[:, g % 2, :]
                    if g >= 2:
                        pool.wait_ge(g_full, G[("po", c, g - 2)] + 1)
                    pool.tensor_scalar(done, src[:, HIST:HIST + CHUNK], 1.0 / w, None, ALU.mult).then_inc(pool_steps, 1)
                    mark()
                    if c == 0:
                        pool.tensor_tensor(done[:, 0:w - 1], src[:, HIST:HIST + w - 1], recip_count[:, 0:w - 1],
                                           ALU.mult).then_inc(pool_steps, 1)
                        mark()
                        pool.tensor_copy(hist[:, g, :], u[:, CHUNK:CHUNK + HIST]).then_inc(pool_steps, 1)
                        mark()
                    pool.tensor_tensor(done, done, u[:, HIST:HIST + CHUNK], ALU.subtract).then_inc(pooled_ready, 1)

            def head_masks(c):
                if c == 0:
                    pool.wait_ge(g_evac, G[("near", 3)] + 1)
                pool.wait_ge(g_full, G[("po", c, 3)] + 1)
                for m in range(32 * c, 32 * c + 32):
                    i, h = divmod(m, HEADS)
                    length = (i + 1) * P
                    near = min(NEAR, length)
                    if h == 0 and i >= 2:
                        pool.wait_ge(mask_ready, i - 1)
                    if m >= 2:
                        pool.wait_ge(masked, m - 1)
                    if h < 2 and length > NEAR:
                        pool.tensor_copy(mask[:, m % 2, 0:length - NEAR], score[:, i % CB, 0:length - NEAR])
                    pool.tensor_tensor(mask[:, m % 2, length - near:length], score[:, i % CB, length - near:length],
                                       near_bias[:, h, NEAR - near:NEAR], ALU.add).then_inc(mask_full, 1)

            def mlp_sum(c):
                base = G[("mlp", c, 0)]
                with pool.Fori(0, GROUPS) as g:
                    for j in range(2 * CB):
                        b, nh = j % CB, j // CB
                        pool.wait_ge(g_evac, g * GUSES + (base + GT + j + 1))
                        part = rows[:, b, nh * 512:nh * 512 + 512]
                        pool.tensor_tensor(part, part, y_stage[:, j % 2, :], ALU.add).then_inc(y_added, 1)

            inverse_std(0)
            inverse_std(1)
            times_gain("emb", 0, xstage[:, 0:CB, :], 1, lambda: pool.wait_ge(g_full, G[("xT", 0, KT - 1)] + 1))
            latents(0)
            times_gain("emb", 1, xstage[:, CB:NB, :], 1, lambda: pool.wait_ge(g_full, G[("xT", 1, KT - 1)] + 1))
            diagonals((2, 3))
            pooling(0)
            latents(1)
            head_masks(0)
            inverse_std(2)
            times_gain("ln1", 0, rows, 2, lambda: pool.wait_ge(g_full, G[("x1T", 0, KT - 1)] + 1))
            diagonals((4, 5, 6, 7))
            mlp_sum(0)
            inverse_std(3)
            times_gain("ln2", 0, rows, 3, lambda: None)
            pooling(1)
            head_masks(1)
            inverse_std(4)
            times_gain("ln1", 1, rows, 4, lambda: pool.wait_ge(g_full, G[("x1T", 1, KT - 1)] + 1))
            mlp_sum(1)
            inverse_std(5)
            times_gain("ln2", 1, rows, 5, lambda: None)

        @block.vector
        def _(dve):
            n_steps = [0]

            def chain(ins):
                n_steps[0] += 1
                ins.then_inc(dve_steps, 1)
                dve.wait_ge(dve_steps, n_steps[0])

            def normalize(l, tiles, ready):
                for b in range(CB):
                    ready(b)
                    nc.vector.bn_stats(stats[:, b, 0:6], tiles[:, b, 0:512])
                    chain(nc.vector.bn_stats(stats[:, b, 6:12], tiles[:, b, 512:1024]))
                    nc.vector.bn_aggr(mean_var[:, 4 * l + b, :], stats[:, b, :]).then_inc(stats_ready, 1)
                for b in range(CB):
                    n = 4 * l + b
                    dve.wait_ge(rstd_ready, n + 1)
                    nc.vector.tensor_scalar(tiles[:, b, :], tiles[:, b, :], mean_var[:, n, 0:1], rstd[:, n:n + 1],
                                            ALU.subtract, ALU.mult).then_inc(xhat_ready, 1)

            def add_scores(i):
                length = (i + 1) * P
                s = score[:, i % CB, 0:length]
                for h in range(HEADS):
                    n = 8 * (i - 2) + h
                    dve.wait_ge(relu_ready, n + 1)
                    if h == 0:
                        nc.vector.tensor_scalar(s, relu_sb[:, n % 2, 0:length], idx_w[:, i, h:h + 1], None, ALU.mult)\
                            .then_inc(score_added, 1)
                    else:
                        dve.wait_ge(score_added, n)
                        nc.vector.scalar_tensor_tensor(out=s, in0=relu_sb[:, n % 2, 0:length],
                                                       scalar=idx_w[:, i, h:h + 1], in1=s, op0=ALU.mult, op1=ALU.add)\
                            .then_inc(score_added, 1)

            def select(i):
                length = (i + 1) * P
                s = score[:, i % CB, 0:length]
                w = work[:, 0:length]
                rounds = TOPK // 8
                first = (2 * rounds + 1) * (i - 2)
                dve.wait_ge(diag_masked, i - 1)
                nc.vector.tensor_copy(w, s).then_inc(topk_steps, 1)
                with dve.Fori(0, rounds) as r:
                    dve.wait_ge(topk_steps, 2 * r + (first + 1))
                    dve.sem_inc(topk_turn, 1)
                    nc.vector.max(top8[:, :], w).then_inc(topk_steps, 1)
                    dve.wait_ge(topk_steps, 2 * r + (first + 2))
                    dve.sem_inc(topk_turn, 1)
                    nc.vector.match_replace(w, top8[:, :], w, TAKEN).then_inc(topk_steps, 1)
                dve.wait_ge(topk_steps, first + 2 * rounds + 1)
                chain(nc.vector.tensor_tensor(s, w, s, ALU.is_equal))
                nc.vector.tensor_scalar(s, s, NEG, None, ALU.mult).then_inc(mask_ready, 1)

            def mask_logits(m):
                i, h = divmod(m, HEADS)
                length = (i + 1) * P
                dve.wait_ge(logits_full, m + 1)
                dve.wait_ge(mask_full, m + 1)
                if m >= 2:
                    i2 = (m - 2) // HEADS
                    dve.wait_ge(g_full, G[("tr", m - 2, (i2 + 4) // 4 - 1)] + 1)
                nc.vector.tensor_tensor_reduce(logit[:, m % 2, 0:length], wide[m % 2][:, 0:length],
                                               mask[:, m % 2, 0:length], 1.0, TAKEN, ALU.add, ALU.max,
                                               row_max[:, m % 2:m % 2 + 1]).then_inc(masked, 1)
                dve.wait_ge(masked, m + 1)
                nc.vector.tensor_scalar(neg_max[:, m % 2:m % 2 + 1], row_max[:, m % 2:m % 2 + 1], -1.0, None,
                                        ALU.mult).then_inc(neg_max_ready, 1)

            def scale_heads(i):
                dve.wait_ge(exp_ready, 8 * i + 8)
                chain(nc.vector.reciprocal(exp_rec[:, i % 2, :], exp_sum[:, i % 2, :]))
                dve.wait_ge(g_evac, G[("uv", 4 * i + 3)] + 1)
                a = att[:, i % 2, :].rearrange("p (h d) -> p h d", h=HEADS)
                nc.vector.tensor_tensor(a, a, exp_rec[:, i % 2, :].unsqueeze(2).to_broadcast([P, HEADS, HD]), ALU.mult)\
                    .then_inc(att_ready, 1)

            def attention(c):
                for step in range(32 * c, 32 * c + 32 + 5):
                    if step < 32 * c + 32:
                        mask_logits(step)
                    if step % HEADS == 3 and step - 11 >= 32 * c:
                        scale_heads((step - 11) // HEADS)

            def add_residual(c):
                dve.wait_ge(rows_in, 16 * CB * (c + 1))
                for nh in range(2):
                    for b in range(CB):
                        n = 8 * c + 4 * nh + b
                        dve.wait_ge(wo_full, n + 1)
                        part = rows[:, b, nh * 512:nh * 512 + 512]
                        nc.vector.scalar_tensor_tensor(out=part, in0=part, scalar=ALPHA,
                                                       in1=wide[b // 2][:, (b % 2) * 512:(b % 2) * 512 + 512],
                                                       op0=ALU.mult, op1=ALU.add).then_inc(wo_added, 1)

            dve.wait_ge(counts_ready, 1)
            nc.vector.reciprocal(recip_count[:, :], count[:, :]).then_inc(counts_ready, 1)
            normalize(0, xstage[:, 0:CB, :], lambda b: dve.wait_ge(x_in[b], 16))
            normalize(1, xstage[:, CB:NB, :], lambda b: dve.wait_ge(x_in[CB + b], 16))
            add_scores(2)
            add_scores(3)
            select(2)
            select(3)
            dve.wait_ge(masks01_ready, 2)
            attention(0)
            add_residual(0)
            normalize(2, rows, lambda b: dve.wait_ge(wo_added, 8 * 0 + 4 + b + 1))
            for i in range(CB, NB):
                add_scores(i)
            for i in range(CB, NB):
                select(i)
            normalize(3, rows, lambda b: dve.wait_ge(y_added, 2 + 2 * CB * GROUPS))
            attention(1)
            add_residual(1)
            normalize(4, rows, lambda b: dve.wait_ge(wo_added, 8 * 1 + 4 + b + 1))
            normalize(5, rows, lambda b: dve.wait_ge(y_added, 2 + 2 * 2 * CB * GROUPS))

        @block.scalar
        def _(act):
            def full(name):
                act.wait_ge(g_full, G[name] + 1)

            def copy_out(name, out_ap, in_ap, func=ACT.Copy, **kw):
                full(name)
                nc.scalar.activation(out_ap, in_ap, func, **kw).then_inc(g_evac, 1)

            def transposed(c, what, g, b):
                for k in range(KT):
                    copy_out((what, c, k), xT[c][:, k, :], bank((what, c, k))[:, :], ACT.Identity,
                             scale=g[:, k:k + 1], bias=b[:, k:k + 1])

            def row_parts(c):
                for b in range(CB * c, CB * c + CB):
                    if b >= 2:
                        act.wait_ge(lat_ready, b - 1)
                    full(("row", b))
                    ps = bank(("row", b))
                    nc.scalar.activation(craw[:, b % 2, :], ps[:, 0:LAT], ACT.Copy).then_inc(craw_ready, 1)
                    nc.scalar.activation(idx_w[:, b, :], ps[:, LAT:ROWW], ACT.Copy, scale=HEADS ** -0.5).then_inc(g_evac, 1)
                    act.wait_ge(craw_ready, b + 1)
                    nc.scalar.activation(csq[:, :], craw[:, b % 2, :], ACT.Square, accum_out=csum[:, b:b + 1])\
                        .then_inc(csum_ready, 1)

            def keys_queries(c):
                copy_out(("ik", c), ikT[:, c * CHUNK:(c + 1) * CHUNK], bank(("ik", c))[:, :])
                if c == 1:
                    act.wait_ge(dots_full, 16)
                for p in range(4):
                    copy_out(("iq", c, p), iqT[:, p, :], bank(("iq", c, p))[:, :], scale=HD ** -0.5)

            def relus(blocks):
                for i in blocks:
                    for h in range(HEADS):
                        n = 8 * (i - 2) + h
                        act.wait_ge(dots_full, n + 1)
                        if n >= 2:
                            act.wait_ge(score_added, n - 1)
                        nc.scalar.activation(relu_sb[:, n % 2, 0:(i + 1) * P], wide[n % 2][:, 0:(i + 1) * P], ACT.Relu)\
                            .then_inc(relu_ready, 1)

            def branch(c):
                if c == 0:
                    act.wait_ge(spilled, 16 * NB)
                else:
                    act.wait_ge(y_added, 2 + 2 * CB * GROUPS)
                for name in branches(c):
                    if name[0] == "q":
                        copy_out(name, qT[:, name[2] % 2, :], bank(name)[:, :])
                    elif name[0] == "ql":
                        copy_out(name, qlatT[:, name[2], :], bank(name)[:, :], scale=HD ** -0.5)
                    elif name[0] == "u":
                        if name[2] >= 2:
                            act.wait_ge(pooled_ready, 4 * c + name[2] - 1)
                        copy_out(name, uT[:, name[2] % 2, HIST:HIST + CHUNK], bank(name)[:, :])
                    else:
                        copy_out(name, mixT[:, name[2], :], bank(name)[:, :], scale=pscale[:, name[2]:name[2] + 1])

            def exps(m):
                i, h = divmod(m, HEADS)
                act.wait_ge(neg_max_ready, m + 1)
                p = logit[:, m % 2, 0:(i + 1) * P]
                nc.scalar.activation(p, p, ACT.Exp, bias=neg_max[:, m % 2:m % 2 + 1],
                                     accum_out=exp_sum[:, i % 2, h:h + 1]).then_inc(exp_ready, 1)

            def attention(c):
                lo, hi = 32 * c, 32 * c + 32
                exps(lo)
                for step in range(lo, lo + LAST_STEP):
                    if step + 1 < hi:
                        exps(step + 1)
                    for name in attention_step(c, step):
                        ps = bank(name)
                        if name[0] == "tr":
                            m, t = name[1], name[2]
                            i = m // HEADS
                            n = min(4, i + 1 - 4 * t)
                            copy_out(name, probsT[:, m // 2 % 2, 4 * t:4 * t + n, m % 2, :],
                                     ps[:, 0:n * P].rearrange("p (k q) -> p k q", k=n))
                        elif name[0] == "pv":
                            copy_out(name, oT[:, :, :], ps[:, 0:2 * P].rearrange("p (h q) -> p h q", h=2))
                        elif name[0] == "uv":
                            i, pair = divmod(name[1], 4)
                            copy_out(name, att[:, i % 2, pair * P:pair * P + P], ps[:, 0:P])
                        else:
                            i = name[1]
                            copy_out(name, mixT[:, 4:8, i % CB * P:i % CB * P + P],
                                     ps[:, :].rearrange("p (k q) -> p k q", k=4))

            def mlp(c):
                base = G[("mlp", c, 0)]
                if c == 0:
                    act.wait_ge(score_added, 48)
                with act.Fori(0, GROUPS) as g:
                    for t in range(GT):
                        act.wait_ge(g_full, g * GUSES + (base + t + 1))
                        nc.scalar.activation(relu_h[:, t % 2, :], g_bank[(base + t) % 4][:, :], ACT.Relu).then_inc(g_evac, 1)
                        act.wait_ge(g_evac, g * GUSES + (base + t + 1))
                        nc.scalar.activation(hT[:, t, :], relu_h[:, t % 2, :], ACT.Square).then_inc(h_ready, 1)
                    for j in range(2 * CB):
                        act.wait_ge(g_full, g * GUSES + (base + GT + j + 1))
                        act.wait_ge(y_added, g * (2 * CB) + (2 * CB * GROUPS * c + j + 1))
                        nc.scalar.activation(y_stage[:, j % 2, :], g_bank[(base + GT + j) % 4][:, :], ACT.Copy)\
                            .then_inc(g_evac, 1)

            copy_out("vecs", vecs[:, :], bank("vecs")[:, 0:36])
            copy_out("wuk", wukT[:, :, :], bank("wuk")[:, :].rearrange("p (k c) -> p k c", k=4))
            full("bias")
            nc.scalar.activation(bias_row[:, :], bank("bias")[0:HEADS, 0:FWIN], ACT.Copy).then_inc(g_evac, 1)
            act.wait_ge(g_evac, G["bias"] + 1)
            act.sem_inc(bias_row_ready, 1)
            transposed(0, "xT", emb_g, emb_b)
            row_parts(0)
            copy_out(("cT", 0), latT[:, 0:CHUNK], bank(("cT", 0))[:, :])
            keys_queries(0)
            transposed(1, "xT", emb_g, emb_b)
            for n in range(4):
                copy_out(("near", n), near_bias[:, 2 * n:2 * n + 2, :],
                         bank(("near", n))[:, :].rearrange("p (h n) -> p h n", h=2))
            relus((2, 3))
            branch(0)
            row_parts(1)
            copy_out(("cT", 1), latT[:, CHUNK:S], bank(("cT", 1))[:, :])
            keys_queries(1)
            attention(0)
            transposed(0, "x1T", l1_g, l1_b)
            relus((4, 5, 6, 7))
            mlp(0)
            branch(1)
            attention(1)
            transposed(1, "x1T", l1_g, l1_b)
            mlp(1)

        @block.tensor
        def _(pe):
            def free(name):
                if G[name] >= 4:
                    pe.wait_ge(g_evac, G[name] - 3)

            def transposes(name, parts):
                free(name)
                ps = bank(name)
                for n, part in enumerate(parts):
                    rows_in_part = part.shape[0]
                    last = nc.tensor.transpose(ps[:, n * P:n * P + rows_in_part] if rows_in_part == P
                                               else ps[:, 0:rows_in_part], part,
                                               ident[0:rows_in_part, 0:rows_in_part])
                last.then_inc(g_full, 1)

            def evacuated(name):
                pe.wait_ge(g_evac, G[name] + 1)

            def x_transposes(c, what, tiles, l):
                pe.wait_ge(xhat_ready, 4 * l + CB)
                for k in range(KT):
                    transposes((what, c, k), [tiles[:, b, k * P:(k + 1) * P] for b in range(CB)])

            def project(name, c):
                unit_arrived_in(name)
                free(name)
                w = unit_tile(name)[:, :].rearrange("p (k n) -> p k n", k=KT)
                for k in range(KT):
                    last = nc.tensor.matmul(bank(name)[:, :], w[:, k, :], xT[c][:, k, :], start=(k == 0), stop=(k == KT - 1))
                last.then_inc(g_full, 1)

            def unit_arrived_in(name):
                n = U[name]
                loads = n // 4 + 1 + sum(1 for k in (U[("ik", 0)], U[("ik", 1)]) if k % 4 == n % 4 and k <= n)
                pe.wait_ge(ring_in[n % 4], 16 * loads)

            def row_projections(c):
                if c == 0:
                    pe.wait_ge(roww_in, 48)
                for b in range(CB):
                    name = ("row", CB * c + b)
                    free(name)
                    for k in range(KT):
                        last = nc.tensor.matmul(bank(name)[:, 0:ROWW], xT[c][:, k, b * P:(b + 1) * P], roww[:, k, :],
                                                start=(k == 0), stop=(k == KT - 1))
                    last.then_inc(g_full, 1)

            def latent_transposes(c):
                pe.wait_ge(lat_ready, CB * (c + 1))
                transposes(("cT", c), [lat[:, CB * c + b, :] for b in range(CB)])

            def dots(blocks):
                for i in blocks:
                    length = (i + 1) * P
                    for h in range(HEADS):
                        n = 8 * (i - 2) + h
                        if n >= 2:
                            pe.wait_ge(relu_ready, n - 1)
                        half = slice((h % 2) * HD, (h % 2) * HD + HD)
                        for k0 in range(0, length, 512):
                            k1 = min(length, k0 + 512)
                            last = nc.tensor.matmul(wide[n % 2][:, k0:k1], iqT[half, h // 2, i % CB * P:i % CB * P + P],
                                                    ikT[half, k0:k1], start=True, stop=True)
                        last.then_inc(dots_full, 1)

            def branch(c):
                for name in branches(c):
                    if name[0] in ("q", "u"):
                        project(name, c)
                    elif name[0] == "ql":
                        h = name[2]
                        evacuated(("q", c, h // 2))
                        free(name)
                        half = slice((h % 2) * HD, (h % 2) * HD + HD)
                        nc.tensor.matmul(bank(name)[:, :], wukT[half, h // 2, :], qT[half, h // 2 % 2, :],
                                         start=True, stop=True).then_inc(g_full, 1)
                    else:
                        g = name[2]
                        pe.wait_ge(pooled_ready, 4 * c + g + 1)
                        free(name)
                        nc.tensor.matmul(bank(name)[:, :], poolw[:, g, :], pooledT[:, g % 2, :],
                                         start=True, stop=True).then_inc(g_full, 1)

            def logits(m):
                i, h = divmod(m, HEADS)
                length = (i + 1) * P
                if m >= 2:
                    pe.wait_ge(masked, m - 1)
                for k0 in range(0, length, 512):
                    k1 = min(length, k0 + 512)
                    last = nc.tensor.matmul(wide[m % 2][:, k0:k1], qlatT[:, h, i % CB * P:i % CB * P + P], latT[:, k0:k1],
                                            start=True, stop=True)
                last.then_inc(logits_full, 1)

            def attention(c):
                lo, hi = 32 * c, 32 * c + 32
                evacuated(("ql", c, 7))
                pe.wait_ge(relu_ready, 16 if c == 0 else 48)
                logits(lo)
                logits(lo + 1)
                for step in range(lo, lo + LAST_STEP):
                    for name in attention_step(c, step):
                        if name[0] == "tr":
                            m, t = name[1], name[2]
                            i = m // HEADS
                            pe.wait_ge(exp_ready, m + 1)
                            transposes(name, [logit[:, m % 2, k * P:(k + 1) * P] for k in range(4 * t, min(4 * t + 4, i + 1))])
                        elif name[0] == "pv":
                            v = name[1]
                            i = v // 4
                            m = 2 * v + 1
                            evacuated(("tr", m, (i + 4) // 4 - 1))
                            free(name)
                            for k in range(i + 1):
                                last = nc.tensor.matmul(bank(name)[:, 0:2 * P], lat[:, k, :],
                                                        probsT[:, v % 2, k, :, :].rearrange("p h q -> p (h q)"),
                                                        start=(k == 0), stop=(k == i))
                            last.then_inc(g_full, 1)
                        elif name[0] == "uv":
                            v = name[1]
                            evacuated(("pv", v))
                            free(name)
                            for e in range(2):
                                h = 2 * (v % 4) + e
                                last = nc.tensor.matmul(bank(name)[:, e * HD:e * HD + HD], oT[:, e, :],
                                                        wuv[:, h * HD:h * HD + HD], start=True, stop=True)
                            last.then_inc(g_full, 1)
                        else:
                            i = name[1]
                            pe.wait_ge(att_ready, i + 1)
                            transposes(name, [att[:, i % 2, k * P:(k + 1) * P] for k in range(4)])
                    if step + 2 < hi:
                        logits(step + 2)

            def output_projection(c):
                evacuated(("aT", CB * c + CB - 1))
                evacuated(("po", c, 3))
                pe.wait_ge(masked, 32 * c + 32)
                for nh in range(2):
                    for u in range(4):
                        name = ("wo", c, nh, u)
                        unit_arrived_in(name)
                        w = unit_tile(name)[:, :].rearrange("p (k n) -> p k n", k=2)
                        for b in range(CB):
                            if nh == 1 and u == 0:
                                pe.wait_ge(wo_added, 8 * c + b + 1)
                            for k in range(2):
                                last = nc.tensor.matmul(wide[b // 2][:, (b % 2) * 512:(b % 2) * 512 + 512],
                                                        mixT[:, 2 * u + k, b * P:(b + 1) * P], w[:, k, :],
                                                        start=(u == 0 and k == 0), stop=(u == 3 and k == 1))
                            if u == 3:
                                last.then_inc(wo_full, 1)
                        if u < 3:
                            last.then_inc(wo_used, 1)

            def mlp(c):
                base = G[("mlp", c, 0)]
                first = U[("up", c, 0)]
                evacuated(("x1T", c, KT - 1))
                with pe.Fori(0, GROUPS) as g:
                    for t in range(GT):
                        slot = (first + t) % 4
                        extra = sum(1 for k in (U[("ik", 0)], U[("ik", 1)]) if k % 4 == slot)
                        pe.wait_ge(ring_in[slot], g * (16 * GT // 4) + 16 * ((first + t) // 4 + 1 + extra))
                        pe.wait_ge(g_evac, g * GUSES + (base + t - 3))
                        w = wring[slot][:, :].rearrange("p (k n) -> p k n", k=KT)
                        for k in range(KT):
                            last = nc.tensor.matmul(g_bank[(base + t) % 4][:, :], w[:, k, :], xT[c][:, k, :],
                                                    start=(k == 0), stop=(k == KT - 1))
                        last.then_inc(g_full, 1)
                    pe.wait_ge(wdown_in, g * 16 + 16 * (GROUPS * c + 1))
                    pe.wait_ge(h_ready, g * GT + (GT * GROUPS * c + GT))
                    for j in range(2 * CB):
                        b, nh = j % CB, j // CB
                        pe.wait_ge(g_evac, g * GUSES + (base + GT + j - 3))
                        for f in range(GT):
                            last = nc.tensor.matmul(g_bank[(base + GT + j) % 4][:, :], hT[:, f, b * P:(b + 1) * P],
                                                    wdown_sb[:, f, nh * 512:nh * 512 + 512],
                                                    start=(f == 0), stop=(f == GT - 1))
                        last.then_inc(g_full, 1)

            pe.wait_ge(ident_ready, 2)
            pe.wait_ge(small_in, 16 * 8)
            transposes("vecs", [vec_rows[:, :]])
            transposes("wuk", [wuk_raw[:, k * P:(k + 1) * P] for k in range(4)])
            nc.tensor.matmul(bank("bias")[0:HEADS, 0:FWIN], relb[:, :], hots[:, :], start=True, stop=True).then_inc(g_full, 1)
            x_transposes(0, "xT", xstage[:, 0:CB, :], 0)
            evacuated(("xT", 0, KT - 1))
            row_projections(0)
            latent_transposes(0)
            project(("ik", 0), 0)
            for p in range(4):
                project(("iq", 0, p), 0)
            x_transposes(1, "xT", xstage[:, CB:NB, :], 1)
            pe.wait_ge(bias_in, 16)
            for n in range(4):
                free(("near", n))
                nc.tensor.matmul(bank(("near", n))[:, :], flip[:, :], near_up[:, 2 * n:2 * n + 2, :].rearrange("p h n -> p (h n)"),
                                 start=True, stop=True).then_inc(g_full, 1)
            evacuated(("iq", 0, 3))
            dots((2, 3))
            pe.wait_ge(late_in, 32)
            branch(0)
            row_projections(1)
            latent_transposes(1)
            project(("ik", 1), 1)
            for p in range(4):
                project(("iq", 1, p), 1)
            attention(0)
            output_projection(0)
            x_transposes(0, "x1T", rows, 2)
            evacuated(("iq", 1, 3))
            pe.wait_ge(wo_added, 8)
            dots((4, 5, 6, 7))
            mlp(0)
            branch(1)
            attention(1)
            output_projection(1)
            x_transposes(1, "x1T", rows, 4)
            mlp(1)


_INS = ["x", "emb_ln_g", "emb_ln_b", "rel_bias", "w_in", "pool_w", "pool_scale", "kv_norm_g", "w_uk", "w_uv", "w_o",
        "ln1_g", "ln1_b", "w_up", "w_down", "ln2_g", "ln2_b"]


def kernel(**inputs):
    import concourse.bacc as bacc
    from concourse.bass_utils import run_bass_kernel_spmd

    nc = bacc.Bacc("TRN2", target_bir_lowering=False, num_devices=1)
    arrays, args = {}, []
    for name in _INS:
        a = np.ascontiguousarray(inputs[name])
        arrays[f"in_{name}"] = a
        args.append(nc.dram_tensor(f"in_{name}", a.shape, mybir.dt.from_np(a.dtype), kind="ExternalInput").ap())
    arrays["in_buckets"] = bucket_differences()
    args.append(nc.dram_tensor("in_buckets", (NBUCKET, FWIN), F32, kind="ExternalInput").ap())
    args.append(nc.dram_tensor("normalized_rows", (S, D), F32).ap())
    args.append(nc.dram_tensor("bias_rows", (HEADS, FWIN), F32).ap())
    args.append(nc.dram_tensor("out_0", (1, S, D), F32, kind="ExternalOutput").ap())
    layer(nc, *args)
    r = run_bass_kernel_spmd(nc, [arrays], core_ids=[0])
    return r.results[0]["out_0"]
```

```python
from contextlib import ExitStack

import numpy as np

import concourse.bass as bass
from concourse import mybir

F32 = mybir.dt.float32
F32R = mybir.dt.float32r
ALU = mybir.AluOpType
ACT = mybir.ActivationFunctionType

P = 128
S = 1024
D = 1024
KT = D // P
CHUNK = 512
CB = CHUNK // P
NB = S // P
HEADS = 8
HD = 64
LAT = 128
WINDOWS = (2, 4, 8, 16)
TOPK = 256
FF = 4 * D
NBUCKET = 32
MAX_DIST = 128
ALPHA = 2.0 ** 0.25
EPS = 1e-5
NEG = -1.0e30
TAKEN = -3.0e38
HIST = 16
NEAR = 2 * P
FWIN = NEAR + P

COL_U, COL_Q, COL_C, COL_IQ = 0, 512, 1024, 1152
COL_IK = COL_IQ + HEADS * HD
COL_IW = COL_IK + HD
KEYW = HD + HEADS
GT = 8
GROUPS = FF // P // GT
GUNITS = 2 * GT
KB = 1024


def bucket_differences():
    n = np.maximum(NEAR - 1 - np.arange(FWIN), 0)
    exact = NBUCKET // 2
    large = exact + (np.log(np.maximum(n, 1) / exact) / np.log(MAX_DIST / exact) * exact).astype(np.int64)
    bucket = np.where(n < exact, n, np.minimum(large, NBUCKET - 1))
    hot = (np.arange(NBUCKET)[:, None] == bucket[None, :]).astype(np.float32)
    hot[NBUCKET - 1] -= 1.0
    return hot


def chunk_uses(c):
    uses = [("ik", c), ("c", c), ("iq", c, 0), ("iw", c), ("cR", c)] + [("iq", c, p) for p in (1, 2, 3)] + [("cT", c)]
    return uses + tokens_queries(c)


def tokens_queries(c):
    order = ("u0 u1 u2 po0 u3 po1 q0 po2 q1 po3 q2 q3", "q0 q1 q2 u0 u1 u2 po0 u3 po1 q3 po2 po3")[c]
    return [(name[:-1], c, int(name[-1])) for name in order.split()]


def psum_uses():

    def attention(c):
        out = []
        for step in range(32 * c, 32 * c + 32 + 5):
            out += attention_step(c, step)
        return out

    names = ["vecs"] + [("xT", 0, k) for k in range(KT)] + ["wuk", "bias"] + chunk_uses(0)
    names += [("near", n) for n in range(4)] + [("ql", 0, h) for h in range(HEADS)]
    names += [("xT", 1, k) for k in range(KT)] + chunk_uses(1)
    for c in range(2):
        if c:
            names += [("ql", 1, h) for h in range(HEADS)]
        names += attention(c) + [("proj", c, nh, b) for nh in range(2) for b in range(CB)]
        names += [("x1T", c, k) for k in range(KT)] + [("mlp", c, n) for n in range(GROUPS * GT)]
    return names


def attention_step(c, step):
    lo, hi = 32 * c, 32 * c + 32
    out = []
    if step < hi:
        i = step // HEADS
        out += [("tr", step, t) for t in range((i + 4) // 4)]
    if step % 2 == 0 and lo <= step - 2 < hi:
        out += [("pv", (step - 2) // 2)]
    if step % 2 == 1 and lo <= step - 3 < hi:
        out += [("uv", (step - 3) // 2)]
    if step % HEADS == 4 and lo <= step - 12 < hi:
        out += [("aT", (step - 12) // HEADS)]
    return out


LAST_STEP = 32 + 5


def layer(nc, x, emb_ln_g, emb_ln_b, rel_bias, w_in, pool_w, pool_scale, kv_norm_g, w_uk, w_uv, w_o,
          ln1_g, ln1_b, w_up, w_down, ln2_g, ln2_b, buckets, spill, bias_rows, out):
    uses = psum_uses()
    G = {name: k for k, name in enumerate(uses)}
    EV = {name: sum(1 for n in uses[:k + 1] if n[0] != "proj") for name, k in G.items()}
    xd = x.rearrange("o (b p) d -> (o b) p d", p=P)
    outd = out.rearrange("o (b p) d -> (o b) p d", p=P)
    spilld = spill.rearrange("(b p) d -> b p d", p=P)
    wind = w_in.rearrange("o (k p) n -> p (o k) n", p=P)
    wod = w_o.rearrange("o (k p) n -> p (o k) n", p=P)
    wupd = w_up.rearrange("o (k p) n -> p (o k) n", p=P)
    wdownd = w_down.rearrange("o (f p) n -> p (o f) n", p=P)

    with ExitStack() as ctx:
        def sb(name, shape, dt=F32):
            return ctx.enter_context(nc.sbuf_tensor(name, shape, dt))

        def sem(name):
            return ctx.enter_context(nc.semaphore(name))

        g_bank = [ctx.enter_context(nc.psum_tensor(f"g_bank{i}", [P, 512], F32)) for i in range(4)]
        wide = [ctx.enter_context(nc.psum_tensor(f"wide{i}", [P, 1024], F32)) for i in range(2)]

        def bank(name):
            return g_bank[G[name] % 4]

        arena_at = -(-nc.sbuf_base // 32) * 32
        sb("arena", [P, (arena_at - nc.sbuf_base + 78 * KB) // 4])

        def part(name, kb, shape, dt=F32):
            return nc.alloc_sbuf_tensor_at(name, shape, dt, offset=arena_at + int(kb * KB))

        xhi = part("xhi", 0, [P, KT, CHUNK], F32R)
        xlo = part("xlo", 16, [P, KT, CHUNK], F32R)
        probsT = part("probsT", 0, [P, 2, NB, 2, P])
        logit = part("logit", 16, [P, 2, S])
        mask = part("mask", 24, [P, 2, S])
        qlatT = part("qlatT", 32, [P, HEADS, CHUNK])
        relu_sb = part("relu_sb", 32, [P, 2, S])
        near_up = part("near_up", 40, [P, HEADS, NEAR])
        wuk_raw = part("wuk_raw", 40, [P, HEADS * HD])
        hots = part("hots", 42, [NBUCKET, FWIN])
        bias_row = part("bias_row", 43.5, [HEADS, FWIN])
        vec_rows = part("vec_rows", 45, [37, P])
        hhi = part("hhi", 32, [P, GT, CHUNK], F32R)
        hlo = part("hlo", 48, [P, GT, CHUNK], F32R)
        iq2 = part("iq2", 48, [P, HEADS, CHUNK], F32R)
        att_hi = part("att_hi", 0, [P, 4, CHUNK], F32R)
        att_lo = part("att_lo", 8, [P, 4, CHUNK], F32R)
        pool_hi = part("pool_hi", 16, [P, 4, CHUNK], F32R)
        pool_lo_part = part("pool_lo", 24, [P, 4, CHUNK], F32R)
        att_outT = part("att_outT", 64, [P, 4, CHUNK])
        uT = part("uT", 64, [P, 2, HIST + CHUNK])
        win = part("win", 68.125, [P, 2, HIST + CHUNK])
        pooledT = part("pooledT", 72.25, [P, 2, CHUNK])
        att = part("att", 72, [P, 2, 512])
        oT = part("oT", 76, [P, 2, P])
        relu_h = part("relu_h", 64, [P, 2, CHUNK])
        h_sq = part("h_sq", 68, [P, CHUNK])
        y_stage = part("y_stage", 70, [P, CB, 512])

        rows = sb("rows", [P, CB, D])
        wring = [sb(f"wring{s}", [P, D]) for s in range(4)]
        whi = [sb(f"whi{s}", [P, D], F32R) for s in range(2)]
        wlo = [sb(f"wlo{s}", [P, D], F32R) for s in range(2)]
        val = sb("val", [P, 2, CHUNK])
        score = sb("score", [P, CB, S])
        work = sb("work", [P, S])
        near_bias = sb("near_bias", [P, HEADS, NEAR])
        qT = sb("qT", [P, 4, CHUNK])
        pool_out = [sb(f"pool_out{c}", [P, 4, CHUNK]) for c in range(2)]
        key_hi = sb("key_hi", [P, S], F32R)
        key_lo = sb("key_lo", [P, S], F32R)
        lat = sb("lat", [P, NB, LAT])
        latT = sb("latT", [P, S])
        gains = sb("gains", [P, 2, D])
        ident = sb("ident", [P, P])
        flip = sb("flip", [P, P])
        wukT = sb("wukT", [P, 4, LAT])
        wuv = sb("wuv", [P, HEADS * HD])
        poolw = sb("poolw", [P, 4, P])
        vecs = sb("vecs", [P, 37])
        relb = sb("relb", [NBUCKET, HEADS])
        recip_count = sb("recip_count", [P, HIST])
        count = sb("count", [P, HIST])
        hist = sb("hist", [P, 4, HIST])
        craw = sb("craw", [P, CB, LAT])
        csq = sb("csq", [P, CB, LAT])
        idx_w = sb("idx_w", [P, NB, HEADS])
        stats = sb("stats", [P, CB, 12])
        mean_var = sb("mean_var", [P, 6 * CB, 2])
        rstd = sb("rstd", [P, 6 * CB])
        shift = sb("shift", [P, 6 * CB])
        power = sb("power", [P, 1])
        csum = sb("csum", [P, NB])
        crstd = sb("crstd", [P, NB])
        top8 = sb("top8", [P, 2, 8])
        row_max = sb("row_max", [P, 2])
        neg_max = sb("neg_max", [P, 2])
        exp_sum = sb("exp_sum", [P, 2, HEADS])
        exp_rec = sb("exp_rec", [P, 2, HEADS])

        def k_columns(w):
            return w[:, :].rearrange("p (k n) -> p k n", k=KT)

        def k_pairs(w):
            return w[:, :].rearrange("p (k n) -> p k n", k=2)

        emb_g, emb_b, l1_g, l1_b = (vecs[:, 8 * n:8 * n + 8] for n in range(4))
        pscale, kv_g = vecs[:, 32:36], vecs[:, 36:37]

        x_in = [sem(f"x_in{b}") for b in range(NB)]
        small_in = sem("small_in")
        late_in = sem("late_in")
        ring_in = [sem(f"ring_in{s}") for s in range(4)]
        gains_in = sem("gains_in")
        wdown_in = sem("wdown_in")
        rows_in = sem("rows_in")
        spilled = sem("spilled")
        bias_out = sem("bias_out")
        bias_in = sem("bias_in")
        stored = sem("stored")
        g_full = sem("g_full")
        g_evac = sem("g_evac")
        bias_row_ready = sem("bias_row_ready")
        ident_ready = sem("ident_ready")
        const_steps = sem("const_steps")
        counts_ready = sem("counts_ready")
        masks01_ready = sem("masks01_ready")
        dve_steps = sem("dve_steps")
        stats_ready = sem("stats_ready")
        bn_ready = sem("bn_ready")
        var_eps = sem("var_eps")
        rstd_ready = sem("rstd_ready")
        shift_ready = sem("shift_ready")
        xhat_ready = sem("xhat_ready")
        x1_hat_ready = sem("x1_hat_ready")
        emb_rows = sem("emb_rows")
        x1_rows = sem("x1_rows")
        out_rows = sem("out_rows")
        hi_ready = sem("hi_ready")
        lo_dve = sem("lo_dve")
        lo_pool = sem("lo_pool")
        key_lo_ready = sem("key_lo_ready")
        iq_lo_ready = sem("iq_lo_ready")
        mix_hi_ready = sem("mix_hi_ready")
        mix_lo_ready = sem("mix_lo_ready")
        x_lo_dve = sem("x_lo_dve")
        x_lo_pool = sem("x_lo_pool")
        h_hi_ready = sem("h_hi_ready")
        h_squared = [sem(f"h_squared{c}") for c in range(2)]
        h_lo_ready = [sem(f"h_lo_ready{c}") for c in range(2)]
        unit_used = sem("unit_used")
        wide_full = sem("wide_full")
        y_evac = sem("y_evac")
        csum_ready = sem("csum_ready")
        crstd_ready = sem("crstd_ready")
        lat_ready = sem("lat_ready")
        dots_full = sem("dots_full")
        relu_ready = sem("relu_ready")
        score_added = sem("score_added")
        diag_masked = sem("diag_masked")
        topk_steps = sem("topk_steps")
        topk_turn = sem("topk_turn")
        mask_ready = sem("mask_ready")
        pool_steps = sem("pool_steps")
        pooled_ready = sem("pooled_ready")
        mask_full = sem("mask_full")
        logits_full = sem("logits_full")
        masked = sem("masked")
        neg_max_ready = sem("neg_max_ready")
        exp_ready = sem("exp_ready")
        att_ready = sem("att_ready")
        wo_used = sem("wo_used")
        wo_added = sem("wo_added")
        y_added = sem("y_added")

        units = []
        for c in range(2):
            units += [("ik", c), ("c", c)] + [("iq", c, p) for p in range(4)]
            units += [name for name in tokens_queries(c) if name[0] != "po"]
        for c in range(2):
            units += [("wo", c, nh, u) for nh in range(2) for u in range(4)]
            units += [("mlp", c, j) for j in range(GROUPS * GUNITS)]
        U = {name: n for n, name in enumerate(units)}
        dve_lo = [n for n in units if n in (("ik", 0), ("c", 0), ("iq", 0, 0), ("iq", 0, 1), ("iq", 0, 2), ("iq", 0, 3))
                  or n[:2] == ("mlp", 1)]
        pool_lo = [n for n in units if n not in dve_lo]
        LO = {name: (lo_dve, n + 1) for n, name in enumerate(dve_lo)}
        LO.update({name: (lo_pool, n + 1) for n, name in enumerate(pool_lo)})

        def arrivals(n):
            return 16 * (n // 4 + 1)

        def parts_of(name, w):
            return k_columns(w)[:, :, 0:KEYW] if name[0] == "ik" else w[:, :]

        def wait_unit_done(eng, c, g, j):
            if j < GT:
                eng.wait_ge(g_full, g * GT + (G[("mlp", c, 0)] + j + 1))
                return
            nh, u = divmod(j - GT, 4)
            if u < 3:
                eng.wait_ge(unit_used, g * 6 + (6 * GROUPS * c + 3 * nh + u + 1))
            else:
                eng.wait_ge(wide_full, g * 8 + (8 * GROUPS * c + 4 * nh + 4))

        def wait_product(eng, name):
            if name[0] == "mlp":
                wait_unit_done(eng, name[1], name[2] // GUNITS, name[2] % GUNITS)
            elif name[0] != "wo":
                eng.wait_ge(g_full, G[name] + 1)
            elif name[3] == 3:
                eng.wait_ge(g_full, G[("proj", name[1], name[2], CB - 1)] + 1)
            else:
                eng.wait_ge(wo_used, 6 * name[1] + 3 * name[2] + name[3] + 1)

        def split_lo(eng, name, sem_lo, at=None):
            n = U[name]
            eng.wait_ge(hi_ready, n + 1 if at is None else at)
            eng.tensor_tensor(parts_of(name, wlo[n % 2]), parts_of(name, wring[n % 4]),
                              parts_of(name, whi[n % 2]).bitcast(F32), ALU.subtract).then_inc(sem_lo, 1)

        EMB0, EMB1, LN1_0, LN2_0, LN1_1, LN2_1 = range(6)

        block = ctx.enter_context(nc.Block())

        @block.sync
        def _(sp):
            def load_unit(name):
                n = U[name]
                slot = wring[n % 4]
                if n >= 4:
                    sp.wait_ge(*LO[units[n - 4]])
                if name[0] == "wo":
                    _, c, nh, u = name
                    sp.dma_start(k_pairs(slot), wod[:, 2 * u:2 * u + 2, nh * 512:nh * 512 + 512]).then_inc(ring_in[n % 4], 16)
                elif name[0] == "ik":
                    sp.dma_start(parts_of(name, slot), wind[:, :, COL_IK:COL_IK + KEYW]).then_inc(ring_in[n % 4], 16)
                else:
                    col = {"c": COL_C, "iq": COL_IQ, "q": COL_Q, "u": COL_U}[name[0]] + (P * name[2] if name[0] != "c" else 0)
                    sp.dma_start(k_columns(slot), wind[:, :, col:col + P]).then_inc(ring_in[n % 4], 16)

            def load_gains(g, b):
                sp.dma_start(gains[:, 0, :], g.to_broadcast([P, D])).then_inc(gains_in, 16)
                sp.dma_start(gains[:, 1, :], b.to_broadcast([P, D])).then_inc(gains_in, 16)

            def load_mlp(c):
                first = U[("mlp", c, 0)]
                sem_lo, lo_base = LO[("mlp", c, 0)]
                sp.wait_ge(*LO[units[first - 1]])
                with sp.Fori(0, GROUPS) as g:
                    for j in range(GUNITS):
                        slot = (first + j) % 4
                        sp.wait_ge(sem_lo, g * GUNITS + (lo_base - 1 + j - 4 + 1))
                        if j < GT:
                            src = wupd[:, :, bass.ds(g * (GT * P) + j * P, P)]
                            dst = k_columns(wring[slot])
                        else:
                            nh, u = divmod(j - GT, 4)
                            src = wdownd[:, bass.ds(g * GT + 2 * u, 2), nh * 512:nh * 512 + 512]
                            dst = k_pairs(wring[slot])
                        sp.dma_start(dst, src).then_inc(ring_in[slot], 16)

            def store(c):
                for b in range(CB):
                    sp.wait_ge(out_rows, CB * c + b + 1)
                    sp.dma_start(outd[CB * c + b], rows[:, b, :]).then_inc(stored, 16)

            def load_units(names):
                for name in names:
                    load_unit(name)

            sp.dma_start(vec_rows[0:8, :], emb_ln_g.rearrange("(k p) -> k p", p=P)).then_inc(small_in, 16)
            sp.dma_start(vec_rows[8:16, :], emb_ln_b.rearrange("(k p) -> k p", p=P)).then_inc(small_in, 16)
            sp.dma_start(vec_rows[16:24, :], ln1_g.rearrange("o (k p) -> (o k) p", p=P)).then_inc(small_in, 16)
            sp.dma_start(vec_rows[24:32, :], ln1_b.rearrange("o (k p) -> (o k) p", p=P)).then_inc(small_in, 16)
            sp.dma_start(vec_rows[32:36, :], pool_scale.rearrange("o (k p) -> (o k) p", p=P)).then_inc(small_in, 16)
            sp.dma_start(vec_rows[36:37, :], kv_norm_g).then_inc(small_in, 16)
            for b in range(CB):
                sp.dma_start(rows[:, b, :], xd[b]).then_inc(x_in[b], 16)
            load_unit(units[0])
            load_unit(units[1])
            load_unit(units[2])
            load_unit(units[3])
            sp.dma_start(wuk_raw[:, :], w_uk.rearrange("o c h d -> (o c) (h d)")).then_inc(late_in, 16)
            sp.dma_start(relb[:, :], rel_bias).then_inc(late_in, 16)
            sp.dma_start(hots[:, :], buckets).then_inc(late_in, 16)
            sp.dma_start(wuv[:, :], w_uv.rearrange("o c h d -> (o c) (h d)")).then_inc(late_in, 16)
            sp.dma_start(poolw[:, :, :], pool_w.rearrange("o g c d -> c (o g) d")).then_inc(late_in, 16)
            load_gains(emb_ln_g.rearrange("(o d) -> o d", o=1), emb_ln_b.rearrange("(o d) -> o d", o=1))
            load_units(units[4:7])
            for b in range(CB):
                sp.wait_ge(emb_rows, b + 1)
                sp.dma_start(spilld[b], rows[:, b, :]).then_inc(spilled, 16)
            sp.wait_ge(spilled, 16 * CB)
            for b in range(CB):
                sp.dma_start(rows[:, b, :], xd[CB + b]).then_inc(x_in[CB + b], 16)
            sp.wait_ge(bias_row_ready, 1)
            sp.dma_start(bias_rows, bias_row[:, :]).then_inc(bias_out, 16)
            sp.wait_ge(bias_out, 16)
            sp.dma_start(near_up[:, :, :], bass.AP(tensor=bias_rows.tensor, offset=0, ap=[[1, P], [FWIN, HEADS], [1, NEAR]])
                         ).then_inc(bias_in, 16)
            load_units(units[7:U[("wo", 0, 1, 0)]])
            for b in range(CB):
                sp.wait_ge(emb_rows, CB + b + 1)
                sp.dma_start(spilld[CB + b], rows[:, b, :]).then_inc(spilled, 16)
            load_gains(ln1_g, ln1_b)
            sp.wait_ge(spilled, 16 * NB)
            for b in range(CB):
                sp.dma_start(rows[:, b, :], spilld[b]).then_inc(rows_in, 16)
            load_units(units[U[("wo", 0, 1, 0)]:U[("mlp", 0, 0)]])
            load_mlp(0)
            load_units(units[U[("wo", 1, 0, 0)]:U[("wo", 1, 1, 0)]])
            sp.wait_ge(x1_rows, CB)
            load_gains(ln2_g, ln2_b)
            store(0)
            load_gains(ln1_g, ln1_b)
            sp.wait_ge(stored, 16 * CB)
            for b in range(CB):
                sp.dma_start(rows[:, b, :], spilld[CB + b]).then_inc(rows_in, 16)
            load_units(units[U[("wo", 1, 1, 0)]:U[("mlp", 1, 0)]])
            load_mlp(1)
            sp.wait_ge(x1_rows, 2 * CB)
            load_gains(ln2_g, ln2_b)
            store(1)
            sp.wait_ge(stored, 16 * NB)

        def pooling(eng, c, link):
            for g, w in enumerate(WINDOWS):
                u = uT[:, g % 2, :]
                eng.wait_ge(g_evac, EV[("u", c, g)])
                link(eng.tensor_copy(u[:, 0:HIST], hist[:, g, :]))
                src, reach = u, 1
                while reach < w:
                    dst = win[:, (reach.bit_length() - 1) % 2, :]
                    link(eng.tensor_tensor(dst[:, reach:HIST + CHUNK], src[:, reach:HIST + CHUNK],
                                           src[:, 0:HIST + CHUNK - reach], ALU.add))
                    src, low, reach = dst, reach, 2 * reach
                    if reach < w:
                        link(eng.tensor_copy(dst[:, 0:low], u[:, 0:low]))
                done = pooledT[:, g % 2, :]
                if g >= 2:
                    eng.wait_ge(g_full, G[("po", c, g - 2)] + 1)
                link(eng.tensor_scalar(done, src[:, HIST:HIST + CHUNK], 1.0 / w, None, ALU.mult))
                if c == 0:
                    link(eng.tensor_tensor(done[:, 0:w - 1], src[:, HIST:HIST + w - 1], recip_count[:, 0:w - 1], ALU.mult))
                    link(eng.tensor_copy(hist[:, g, :], u[:, CHUNK:CHUNK + HIST]))
                eng.tensor_tensor(done, done, u[:, HIST:HIST + CHUNK], ALU.subtract).then_inc(pooled_ready, 1)
                yield g

        def x_lo(eng, what, c, sem_lo):
            for k in range(KT):
                eng.wait_ge(g_evac, EV[(what, c, k)])
                eng.tensor_tensor(xlo[:, k, :], val[:, k % 2, :], xhi[:, k, :].bitcast(F32), ALU.subtract).then_inc(sem_lo, 1)

        def projection_steps():
            return [(nh, u, b) for nh in range(2) for u in range(4) for b in range(CB)]

        def dots_after(c, nh, u, b):
            n = 16 * nh + 4 * u + b
            doubled = (6, 10, 14, 18, 22)
            if c or n > 26:
                return []
            first = 16 + n + sum(1 for d in doubled if d < n)
            return [first, first + 1] if n in doubled else [first]

        def keys_queries_lo(eng, c, link, between=None):
            eng.wait_ge(g_evac, EV[("ik", c)])
            at = slice(c * CHUNK, (c + 1) * CHUNK)
            link(eng.tensor_tensor(key_lo[0:HD, at], val[0:HD, 0, :], key_hi[0:HD, at].bitcast(F32), ALU.subtract))
            eng.tensor_tensor(key_lo[HD:P, at], val[0:HD, 0, :], key_hi[0:HD, at].bitcast(F32), ALU.subtract)                .then_inc(key_lo_ready, 1)
            eng.wait_ge(key_lo_ready, c + 1)
            for p in range(4):
                if between:
                    between(p)
                eng.wait_ge(g_evac, EV[("iq", c, p)])
                parts = []
                for e in range(2):
                    hi_half, lo_half = slice(e * HD, e * HD + HD), slice(HD - e * HD, 2 * HD - e * HD)
                    parts.append((iq2[lo_half, 2 * p + e, :], val[hi_half, p % 2, :], iq2[hi_half, 2 * p + e, :].bitcast(F32)))
                link(eng.tensor_tensor(*parts[0], ALU.subtract))
                eng.tensor_tensor(*parts[1], ALU.subtract).then_inc(iq_lo_ready, 1)
                eng.wait_ge(iq_lo_ready, 4 * c + p + 1)

        def mlp_lo(eng, c, g, last, after=None):
            sem_lo = LO[("mlp", c, 0)][0]
            evacs = EV[("mlp", c, 0)]
            for j in range(GUNITS):
                if not (last and j >= GUNITS - 2):
                    split_lo(eng, ("mlp", c, (j + 2) % GUNITS), sem_lo, g * GUNITS + (U[("mlp", c, 0)] + j + 3))
                if j < GT:
                    eng.wait_ge(h_lo_ready[c], g * GT + (j + 2))
                    eng.wait_ge(g_evac, g * GT + (evacs + j))
                    eng.tensor_tensor(h_sq[:, :], relu_h[:, j % 2, :], relu_h[:, j % 2, :], ALU.mult)\
                        .then_inc(h_squared[c], 1)
                    eng.wait_ge(h_squared[c], g * GT + (j + 1))
                    eng.wait_ge(h_hi_ready, g * GT + (GT * GROUPS * c + j + 1))
                    eng.tensor_tensor(hlo[:, j, :], h_sq[:, :], hhi[:, j, :].bitcast(F32), ALU.subtract)\
                        .then_inc(h_lo_ready[c], 1)
                if after:
                    after(j)

        def emb_gains(eng, c, link):
            eng.wait_ge(gains_in, 32)
            eng.wait_ge(g_full, G[("xT", c, KT - 1)] + 1)
            for b in range(CB):
                link(eng.tensor_tensor(rows[:, b, :], rows[:, b, :], gains[:, 0, :], ALU.mult))
                eng.tensor_tensor(rows[:, b, :], rows[:, b, :], gains[:, 1, :], ALU.add).then_inc(emb_rows, 1)
                yield b

        def x1_gains(eng, c, link):
            eng.wait_ge(gains_in, 32 * (2 if c == 0 else 4))
            for n in range(2):
                link(eng.tensor_scalar(gains[:, n, :], gains[:, n, :], ALPHA, None, ALU.mult))
            eng.wait_ge(g_full, G[("x1T", c, KT - 1)] + 1)
            for b in range(CB):
                link(eng.tensor_tensor(rows[:, b, :], rows[:, b, :], gains[:, 0, :], ALU.mult))
                eng.tensor_tensor(rows[:, b, :], rows[:, b, :], gains[:, 1, :], ALU.add).then_inc(x1_rows, 1)

        @block.gpsimd
        def _(pool):
            pool.memset(ident[:, :], 0.0).then_inc(const_steps, 1)
            pool.wait_ge(const_steps, 1)
            pool.affine_select(out=ident[:, :], in_=ident[:, :], compare_op=ALU.not_equal, fill=1.0, base=0,
                               pattern=[[-1, P]], channel_multiplier=1).then_inc(ident_ready, 1)
            pool.memset(flip[:, :], 0.0).then_inc(const_steps, 1)
            pool.wait_ge(const_steps, 2)
            pool.affine_select(out=flip[:, :], in_=flip[:, :], compare_op=ALU.not_equal, fill=1.0, base=1 - P,
                               pattern=[[1, P]], channel_multiplier=1).then_inc(ident_ready, 1)
            pool.memset(power[:, :], -0.5).then_inc(const_steps, 1)
            pool.sem_inc(y_added, CB)
            pool.sem_inc(h_lo_ready[0], 2)
            pool.iota(count[:, :], pattern=[[1, HIST]], base=1, channel_multiplier=0,
                      allow_small_or_imprecise_dtypes=True).then_inc(counts_ready, 1)
            pool.memset(hist[:, :, :], 0.0).then_inc(const_steps, 1)
            for i in range(2):
                pool.memset(score[:, i, 0:CHUNK], 0.0).then_inc(const_steps, 1)
            pool.wait_ge(const_steps, 6)
            for i in range(2):
                diag = score[:, i, i * P:(i + 1) * P]
                pool.affine_select(out=diag, in_=diag, compare_op=ALU.is_ge, fill=NEG, base=0,
                                   pattern=[[-1, P]], channel_multiplier=1).then_inc(masks01_ready, 1)

            steps = [0]

            def link(ins):
                steps[0] += 1
                ins.then_inc(pool_steps, 1)
                pool.wait_ge(pool_steps, steps[0])

            def inverse_std(l, blocks=range(CB)):
                for b in blocks:
                    n = 4 * l + b
                    pool.wait_ge(stats_ready, n + 1)
                    pool.tensor_scalar(rstd[:, n:n + 1], mean_var[:, n, 1:2], EPS, None, ALU.add).then_inc(var_eps, 1)
                    pool.wait_ge(var_eps, n + 1)
                    pool.tensor_tensor(rstd[:, n:n + 1], rstd[:, n:n + 1], power[:, :], ALU.pow).then_inc(rstd_ready, 1)
                    if l in (LN1_0, LN1_1):
                        pool.wait_ge(rstd_ready, n + 1)
                        pool.tensor_scalar(shift[:, n:n + 1], mean_var[:, n, 0:1], rstd[:, n:n + 1], -1.0, ALU.mult, ALU.mult)\
                            .then_inc(shift_ready, 1)

            def latents_inverse_rms(c):
                at = slice(CB * c, CB * c + CB)
                pool.wait_ge(csum_ready, CB * c + CB)
                link(pool.tensor_scalar(crstd[:, at], csum[:, at], 1.0 / LAT, EPS, ALU.mult, ALU.add))
                pool.tensor_tensor(crstd[:, at], crstd[:, at], power[:, :].to_broadcast([P, CB]), ALU.pow)\
                    .then_inc(crstd_ready, 1)

            def diagonals(blocks):
                for i in blocks:
                    pool.wait_ge(score_added, 8 * (i - 2) + 8)
                    diag = score[:, i % CB, i * P:(i + 1) * P]
                    pool.affine_select(out=diag, in_=diag, compare_op=ALU.is_ge, fill=TAKEN, base=0,
                                       pattern=[[-1, P]], channel_multiplier=1).then_inc(diag_masked, 1)

            def head_masks(c):
                pool.wait_ge(g_full, G[("po", 1, 3)] + 1)
                for m in range(32 * c, 32 * c + 32):
                    i, h = divmod(m, HEADS)
                    length = (i + 1) * P
                    near = min(NEAR, length)
                    if h == 0 and i >= 2:
                        pool.wait_ge(mask_ready, i - 1)
                    if c == 1 and h in (3, 5, 7) and i == CB or (i, h) == (CB + 1, 1):
                        inverse_std(LN2_0, [(m - 35) // 2])
                    if m >= 2:
                        pool.wait_ge(masked, m - 1)
                    if h < 2 and length > NEAR:
                        pool.tensor_copy(mask[:, m % 2, 0:length - NEAR], score[:, i % CB, 0:length - NEAR])
                    pool.tensor_tensor(mask[:, m % 2, length - near:length], score[:, i % CB, length - near:length],
                                       near_bias[:, h, NEAR - near:NEAR], ALU.add).then_inc(mask_full, 1)

            def add_y(c, g, nh):
                pool.wait_ge(x1_rows, CB * c + CB)
                for b in range(CB):
                    pool.wait_ge(y_evac, g * 8 + (8 * GROUPS * c + 4 * nh + b + 1 + CB))
                    piece = rows[:, b, nh * 512:nh * 512 + 512]
                    pool.tensor_tensor(piece, piece, y_stage[:, b, :], ALU.add).then_inc(y_added, 1)

            def lo(*names):
                for name in names:
                    split_lo(pool, name, lo_pool)

            inverse_std(EMB0)
            for b in emb_gains(pool, 0, link):
                pass
            latents_inverse_rms(0)
            lo(*units[U[("u", 0, 0)]:U[("ik", 1)]])
            diagonals((2, 3))
            inverse_std(EMB1)
            lo(("ik", 1), ("c", 1))
            x_lo(pool, "xT", 1, x_lo_pool)
            lo(("iq", 1, 0), ("iq", 1, 1))

            def ahead(p):
                if p == 1:
                    latents_inverse_rms(1)
                unit = units[U[("iq", 1, p)] + 2]
                lo(unit)
                pool.wait_ge(*LO[unit])

            pool.wait_ge(*LO[("iq", 1, 1)])
            keys_queries_lo(pool, 1, link, ahead)
            lo(*units[U[("iq", 1, 3)] + 3:U[("wo", 0, 0, 2)]])
            head_masks(0)
            lo(*units[U[("wo", 0, 0, 2)]:U[("mlp", 0, 0)]])
            inverse_std(LN1_0)
            lo(("mlp", 0, 0), ("mlp", 0, 1))
            diagonals((4, 5, 6, 7))

            def add_at(c, g):
                def after(j):
                    if j in (GT + 3, GT + 7):
                        add_y(c, g, (j - GT) // 4)
                return after

            with pool.Fori(0, GROUPS - 1) as g:
                mlp_lo(pool, 0, g, False, add_at(0, g))
            mlp_lo(pool, 0, GROUPS - 1, True, add_at(0, GROUPS - 1))
            lo(("wo", 1, 0, 0), ("wo", 1, 0, 1))
            head_masks(1)
            lo(*units[U[("wo", 1, 0, 2)]:U[("mlp", 1, 0)]])
            inverse_std(LN1_1)
            x1_gains(pool, 1, link)
            pool.wait_ge(x1_rows, NB)
            with pool.Fori(0, GROUPS - 1) as g:
                add_y(1, g, 0)
                add_y(1, g, 1)
            inverse_std(LN2_1)

        @block.vector
        def _(dve):
            n_steps = [0]

            def chain(ins):
                n_steps[0] += 1
                ins.then_inc(dve_steps, 1)
                dve.wait_ge(dve_steps, n_steps[0])

            def statistics(l, b):
                nc.vector.bn_stats(stats[:, b, 0:6], rows[:, b, 0:512])
                chain(nc.vector.bn_stats(stats[:, b, 6:12], rows[:, b, 512:1024]))
                nc.vector.bn_aggr(mean_var[:, 4 * l + b, :], stats[:, b, :]).then_inc(stats_ready, 1)

            def normalize(l, c):
                for b in range(CB + 1):
                    if b < CB:
                        dve.wait_ge(x_in[CB * c + b], 16)
                        statistics(l, b)
                    if b > 0:
                        n = 4 * l + b - 1
                        dve.wait_ge(rstd_ready, n + 1)
                        nc.vector.tensor_scalar(rows[:, b - 1, :], rows[:, b - 1, :], mean_var[:, n, 0:1], rstd[:, n:n + 1],
                                                ALU.subtract, ALU.mult).then_inc(xhat_ready, 1)

            def out_norm(c, l, blocks=range(CB)):
                dve.wait_ge(gains_in, 32 * (3 if c == 0 else 5))
                for b in blocks:
                    n = 4 * l + b
                    y = rows[:, b, :]
                    chain(nc.vector.scalar_tensor_tensor(out=y, in0=y, scalar=mean_var[:, n, 0:1], in1=gains[:, 0, :],
                                                         op0=ALU.subtract, op1=ALU.mult))
                    dve.wait_ge(rstd_ready, n + 1)
                    nc.vector.scalar_tensor_tensor(out=y, in0=y, scalar=rstd[:, n:n + 1], in1=gains[:, 1, :],
                                                   op0=ALU.mult, op1=ALU.add).then_inc(out_rows, 1)

            def add_score(n):
                i, h = n // HEADS + 2, n % HEADS
                length = (i + 1) * P
                s = score[:, i % CB, 0:length]
                if n == 16:
                    dve.wait_ge(mask_full, 32)
                dve.wait_ge(relu_ready, n + 1)
                if h == 0:
                    nc.vector.tensor_scalar(s, relu_sb[:, n % 2, 0:length], idx_w[:, i, h:h + 1], None, ALU.mult)\
                        .then_inc(score_added, 1)
                else:
                    dve.wait_ge(score_added, n)
                    nc.vector.scalar_tensor_tensor(out=s, in0=relu_sb[:, n % 2, 0:length],
                                                   scalar=idx_w[:, i, h:h + 1], in1=s, op0=ALU.mult, op1=ALU.add)\
                        .then_inc(score_added, 1)

            def mask_of(i, w):
                s = score[:, i % CB, 0:(i + 1) * P]
                chain(nc.vector.tensor_tensor(s, w, s, ALU.is_equal))
                nc.vector.tensor_scalar(s, s, NEG, None, ALU.mult).then_inc(mask_ready, 1)

            def select_pair():
                w = [work[:, 0:3 * P], work[:, 3 * P:7 * P]]
                dve.wait_ge(diag_masked, 2)
                for e in range(2):
                    nc.vector.tensor_copy(w[e], score[:, 2 + e, 0:(3 + e) * P]).then_inc(topk_steps, 1)
                with dve.Fori(0, TOPK // 8) as r:
                    for e in range(2):
                        dve.wait_ge(topk_steps, 4 * r + (1 + e))
                        dve.sem_inc(topk_turn, 1)
                        nc.vector.max(top8[:, e, :], w[e]).then_inc(topk_steps, 1)
                    for e in range(2):
                        dve.wait_ge(topk_steps, 4 * r + (3 + e))
                        dve.sem_inc(topk_turn, 1)
                        nc.vector.match_replace(w[e], top8[:, e, :], w[e], TAKEN).then_inc(topk_steps, 1)
                dve.wait_ge(topk_steps, 2 + 4 * (TOPK // 8))
                for e in range(2):
                    mask_of(2 + e, w[e])

            def select(i):
                length = (i + 1) * P
                s = score[:, i % CB, 0:length]
                w = work[:, 0:length]
                rounds = TOPK // 8
                first = 2 + 4 * rounds + (2 * rounds + 1) * (i - 4)
                dve.wait_ge(diag_masked, i - 1)
                nc.vector.tensor_copy(w, s).then_inc(topk_steps, 1)
                with dve.Fori(0, rounds) as r:
                    dve.wait_ge(topk_steps, 2 * r + (first + 1))
                    dve.sem_inc(topk_turn, 1)
                    nc.vector.max(top8[:, 0, :], w).then_inc(topk_steps, 1)
                    dve.wait_ge(topk_steps, 2 * r + (first + 2))
                    dve.sem_inc(topk_turn, 1)
                    nc.vector.match_replace(w, top8[:, 0, :], w, TAKEN).then_inc(topk_steps, 1)
                dve.wait_ge(topk_steps, first + 2 * rounds + 1)
                mask_of(i, w)

            def mask_logits(m):
                i, h = divmod(m, HEADS)
                length = (i + 1) * P
                dve.wait_ge(logits_full, m + 1)
                dve.wait_ge(mask_full, m + 1)
                if m >= 2:
                    i2 = (m - 2) // HEADS
                    dve.wait_ge(g_full, G[("tr", m - 2, (i2 + 4) // 4 - 1)] + 1)
                nc.vector.tensor_tensor_reduce(logit[:, m % 2, 0:length], wide[m % 2][:, 0:length],
                                               mask[:, m % 2, 0:length], 1.0, TAKEN, ALU.add, ALU.max,
                                               row_max[:, m % 2:m % 2 + 1]).then_inc(masked, 1)
                dve.wait_ge(masked, m + 1)
                nc.vector.tensor_scalar(neg_max[:, m % 2:m % 2 + 1], row_max[:, m % 2:m % 2 + 1], -1.0, None,
                                        ALU.mult).then_inc(neg_max_ready, 1)

            def scale_heads(i):
                dve.wait_ge(exp_ready, 8 * i + 8)
                chain(nc.vector.reciprocal(exp_rec[:, i % 2, :], exp_sum[:, i % 2, :]))
                dve.wait_ge(g_evac, EV[("uv", 4 * i + 3)])
                a = att[:, i % 2, :].rearrange("p (h d) -> p h d", h=HEADS)
                nc.vector.tensor_tensor(a, a, exp_rec[:, i % 2, :].unsqueeze(2).to_broadcast([P, HEADS, HD]), ALU.mult)\
                    .then_inc(att_ready, 1)

            def attention(c):
                for step in range(32 * c, 32 * c + 32 + 5):
                    if step < 32 * c + 32:
                        mask_logits(step)
                    if step % HEADS == 3 and step - 11 >= 32 * c:
                        scale_heads((step - 11) // HEADS)
                    if c == 1 and 33 <= step < 41 and step % 2 == 1:
                        b = (step - 33) // 2
                        dve.wait_ge(y_added, CB + 8 * GROUPS - 4 + b + 1)
                        statistics(LN2_0, b)
                    if c == 1 and 35 <= step < 43 and step % 2 == 1:
                        out_norm(0, LN2_0, [(step - 35) // 2])
                    if step == 32 * c + 32:
                        mix_lo(c, 0)

            def mix_lo(c, n):
                raw, hi_part, lo_part = ((pool_out[c], pool_hi, pool_lo_part), (att_outT, att_hi, att_lo))[n]
                for k in range(4):
                    dve.wait_ge(mix_hi_ready, 8 * c + 4 * n + k + 1)
                    nc.vector.tensor_tensor(lo_part[:, k, :], raw[:, k, :], hi_part[:, k, :].bitcast(F32), ALU.subtract)\
                        .then_inc(mix_lo_ready, 1)

            def add_residual(c, l):
                dve.wait_ge(rows_in, 16 * CB * (c + 1))
                for nh, u, b in projection_steps():
                    n = 8 * c + 4 * nh + b
                    if u == 3:
                        dve.wait_ge(g_full, G[("proj", c, nh, b)] + 1)
                        piece = rows[:, b, nh * 512:nh * 512 + 512]
                        nc.vector.scalar_tensor_tensor(out=piece, in0=piece, scalar=ALPHA, in1=bank(("proj", c, nh, b))[:, :],
                                                       op0=ALU.mult, op1=ALU.add).then_inc(wo_added, 1)
                        dve.wait_ge(wo_added, n + 1)
                        nc.vector.bn_stats(stats[:, b, 6 * nh:6 * nh + 6], piece).then_inc(bn_ready, 1)
                        if nh == 1:
                            dve.wait_ge(bn_ready, n + 1)
                            nc.vector.bn_aggr(mean_var[:, 4 * l + b, :], stats[:, b, :]).then_inc(stats_ready, 1)
                    for d in dots_after(c, nh, u, b):
                        add_score(d)

            def last_products():
                for b in range(CB):
                    n = 16 * GROUPS - 4 + b
                    dve.wait_ge(wide_full, n + 1)
                    add_last(1, b)
                    dve.wait_ge(y_evac, CB + n + 1)
                    statistics(LN2_1, b)
                    if b > 0:
                        out_norm(1, LN2_1, [b - 1])
                out_norm(1, LN2_1, [CB - 1])

            def add_last(nh, b):
                piece = rows[:, b, nh * 512:nh * 512 + 512]
                nc.vector.tensor_tensor(piece, piece, wide[b // 2][:, (b % 2) * 512:(b % 2) * 512 + 512], ALU.add)\
                    .then_inc(y_evac, 1)

            def first_half(j):
                if j == GT + 3:
                    dve.wait_ge(y_added, CB + 16 * GROUPS - 8)
                    for b in range(CB):
                        dve.wait_ge(wide_full, 16 * GROUPS - 8 + b + 1)
                        add_last(0, b)

            dve.sem_inc(h_lo_ready[1], 2)
            dve.wait_ge(counts_ready, 1)
            nc.vector.reciprocal(recip_count[:, :], count[:, :]).then_inc(counts_ready, 1)
            normalize(EMB0, 0)
            split_lo(dve, ("ik", 0), lo_dve)
            x_lo(dve, "xT", 0, x_lo_dve)
            split_lo(dve, ("c", 0), lo_dve)
            split_lo(dve, ("iq", 0, 0), lo_dve)
            keys_queries_lo(dve, 0, chain, lambda p: split_lo(dve, dve_lo[3 + p], lo_dve) if p < 3 else None)
            pooled = pooling(dve, 0, chain)
            for n in range(8):
                add_score(2 * n)
                add_score(2 * n + 1)
                if n < 4:
                    next(pooled)
            normalize(EMB1, 1)
            select_pair()
            gained = emb_gains(dve, 1, chain)
            for g in pooling(dve, 1, chain):
                next(gained)
            dve.wait_ge(masks01_ready, 2)
            attention(0)
            mix_lo(0, 1)
            add_residual(0, LN1_0)
            x_lo(dve, "x1T", 0, x_lo_dve)
            x1_gains(dve, 0, chain)
            for i in range(CB, NB):
                select(i)
            attention(1)
            mix_lo(1, 1)
            add_residual(1, LN1_1)
            split_lo(dve, ("mlp", 1, 0), lo_dve)
            split_lo(dve, ("mlp", 1, 1), lo_dve)
            x_lo(dve, "x1T", 1, x_lo_dve)
            with dve.Fori(0, GROUPS - 1) as g:
                mlp_lo(dve, 1, g, False)
            mlp_lo(dve, 1, GROUPS - 1, True, first_half)
            last_products()

        @block.scalar
        def _(act):
            def full(name):
                act.wait_ge(g_full, G[name] + 1)

            def copy_out(name, out_ap, in_ap, func=ACT.Copy, **kw):
                full(name)
                nc.scalar.activation(out_ap, in_ap, func, **kw).then_inc(g_evac, 1)

            def transposed(c, what, g, b, sem_lo, lo_before):
                for k in range(KT):
                    name = (what, c, k)
                    full(name)
                    if k >= 2:
                        act.wait_ge(sem_lo, lo_before + k - 1)
                    elif (what, c) in (("xT", 1), ("x1T", 0)):
                        act.wait_ge(iq_lo_ready, 4 if what == "xT" else 8)
                    affine = dict(scale=g[:, k:k + 1], bias=b[:, k:k + 1])
                    nc.scalar.activation(val[:, k % 2, :], bank(name)[:, :], ACT.Identity, **affine)
                    nc.scalar.activation(xhi[:, k, :], bank(name)[:, :], ACT.Identity, **affine).then_inc(g_evac, 1)

            def hi(name):
                n = U[name]
                act.wait_ge(ring_in[n % 4], arrivals(n))
                if n >= 2:
                    wait_product(act, units[n - 2])
                nc.scalar.activation(parts_of(name, whi[n % 2]), parts_of(name, wring[n % 4]), ACT.Copy).then_inc(hi_ready, 1)

            def hi_after(name):
                hi(units[U[name] + 2])

            def keys_queries(c):
                hi_after(("ik", c))
                ps = bank(("ik", c))
                at = slice(c * CHUNK, (c + 1) * CHUNK)
                full(("ik", c))
                act.wait_ge(x_lo_pool if c else x_lo_dve, KT)
                nc.scalar.activation(val[0:KEYW, 0, :], ps[0:KEYW, :], ACT.Copy)
                nc.scalar.activation(key_hi[0:HD, at], ps[0:HD, :], ACT.Copy)
                nc.scalar.activation(key_hi[HD:P, at], ps[0:HD, :], ACT.Copy).then_inc(g_evac, 1)
                hi_after(("c", c))
                copy_out(("c", c), val[:, 1, :], bank(("c", c))[:, :])
                for p in range(4):
                    name = ("iq", c, p)
                    hi_after(name)
                    full(name)
                    if p == 0:
                        act.wait_ge(key_lo_ready, c + 1)
                        full(("iw", c))
                    if p >= 2:
                        act.wait_ge(iq_lo_ready, 4 * c + p - 1)
                    ps = bank(name)
                    nc.scalar.activation(val[:, p % 2, :], ps[:, :], ACT.Copy, scale=HD ** -0.5)
                    nc.scalar.activation(iq2[0:HD, 2 * p, :], ps[0:HD, :], ACT.Copy, scale=HD ** -0.5)
                    nc.scalar.activation(iq2[HD:P, 2 * p + 1, :], ps[HD:P, :], ACT.Copy, scale=HD ** -0.5).then_inc(g_evac, 1)
                    if p == 0:
                        copy_out(("iw", c), idx_w[:, CB * c:CB * c + CB, :],
                                 bank(("iw", c))[:, 0:CB * HEADS].rearrange("p (b h) -> p b h", b=CB), scale=HEADS ** -0.5)
                        copy_out(("cR", c), craw[:, :, :], bank(("cR", c))[:, :].rearrange("p (b n) -> p b n", b=CB))
                        act.wait_ge(g_evac, EV[("cR", c)])
                        for b in range(CB):
                            nc.scalar.activation(csq[:, b, :], craw[:, b, :], ACT.Square,
                                                 accum_out=csum[:, CB * c + b:CB * c + b + 1]).then_inc(csum_ready, 1)
                    if p == 2:
                        act.wait_ge(crstd_ready, c + 1)
                        for b in range(CB):
                            nc.scalar.activation(lat[:, CB * c + b, :], craw[:, b, :], ACT.Copy,
                                                 scale=crstd[:, CB * c + b:CB * c + b + 1]).then_inc(lat_ready, 1)
                copy_out(("cT", c), latT[:, c * CHUNK:(c + 1) * CHUNK], bank(("cT", c))[:, :], scale=kv_g)

            def relu_dots(n):
                i = n // HEADS + 2
                act.wait_ge(dots_full, n + 1)
                if n >= 2:
                    act.wait_ge(score_added, n - 1)
                nc.scalar.activation(relu_sb[:, n % 2, 0:(i + 1) * P], wide[n % 2][:, 0:(i + 1) * P], ACT.Relu)\
                    .then_inc(relu_ready, 1)

            def products(c):
                unit = 0
                for name in tokens_queries(c):
                    n = name[2]
                    if name[0] == "po":
                        copy_out(name, pool_out[c][:, n, :], bank(name)[:, :], scale=pscale[:, n:n + 1])
                        continue
                    if c == 0:
                        relu_dots(2 * unit)
                        relu_dots(2 * unit + 1)
                    unit += 1
                    hi_after(name)
                    if name[0] == "q":
                        copy_out(name, qT[:, n, :], bank(name)[:, :])
                        continue
                    if n >= 2:
                        act.wait_ge(pooled_ready, 4 * c + n - 1)
                    copy_out(name, uT[:, n % 2, HIST:HIST + CHUNK], bank(name)[:, :])

            def latent_queries(c):
                for h in range(HEADS):
                    copy_out(("ql", c, h), qlatT[:, h, :], bank(("ql", c, h))[:, :], scale=HD ** -0.5)

            def exps(m):
                i, h = divmod(m, HEADS)
                act.wait_ge(neg_max_ready, m + 1)
                p = logit[:, m % 2, 0:(i + 1) * P]
                nc.scalar.activation(p, p, ACT.Exp, bias=neg_max[:, m % 2:m % 2 + 1],
                                     accum_out=exp_sum[:, i % 2, h:h + 1]).then_inc(exp_ready, 1)

            def attention(c):
                lo, hi = 32 * c, 32 * c + 32
                exps(lo)
                for step in range(lo, lo + LAST_STEP):
                    if step + 1 < hi:
                        exps(step + 1)
                    if step == hi:
                        mix_hi(c, 0)
                    for name in attention_step(c, step):
                        ps = bank(name)
                        if name[0] == "tr":
                            m, t = name[1], name[2]
                            i = m // HEADS
                            n = min(4, i + 1 - 4 * t)
                            copy_out(name, probsT[:, m // 2 % 2, 4 * t:4 * t + n, m % 2, :],
                                     ps[:, 0:n * P].rearrange("p (k q) -> p k q", k=n))
                        elif name[0] == "pv":
                            copy_out(name, oT[:, :, :], ps[:, 0:2 * P].rearrange("p (h q) -> p h q", h=2), scale=kv_g)
                        elif name[0] == "uv":
                            i, pair = divmod(name[1], 4)
                            copy_out(name, att[:, i % 2, pair * P:pair * P + P], ps[:, 0:P])
                        else:
                            i = name[1]
                            copy_out(name, att_outT[:, :, i % CB * P:i % CB * P + P],
                                     ps[:, :].rearrange("p (k q) -> p k q", k=4))

            def mix_hi(c, n):
                raw, part = ((pool_out[c], pool_hi), (att_outT, att_hi))[n]
                act.wait_ge(masked, 32 * c + 32)
                act.wait_ge(g_evac, EV[("aT", CB * c + CB - 1) if n else ("tr", 32 * c + 31, c)])
                for k in range(4):
                    nc.scalar.activation(part[:, k, :], raw[:, k, :], ACT.Copy).then_inc(mix_hi_ready, 1)

            def normalized(c, l):
                for b in range(CB):
                    n = 4 * l + b
                    act.wait_ge(shift_ready, CB * c + b + 1)
                    nc.scalar.activation(rows[:, b, :], rows[:, b, :], ACT.Identity, scale=rstd[:, n:n + 1],
                                         bias=shift[:, n:n + 1]).then_inc(x1_hat_ready, 1)

            def output_projection(c, l):
                mix_hi(c, 1)
                for nh, u, b in projection_steps():
                    if b == CB - 1 and (nh, u) < (1, 2):
                        hi_after(("wo", c, nh, u))
                    for d in dots_after(c, nh, u, b):
                        relu_dots(d)
                normalized(c, l)
                hi(("mlp", c, 0))
                hi(("mlp", c, 1))

            def mlp(c, g, last):
                base, evacs, first = G[("mlp", c, 0)], EV[("mlp", c, 0)], U[("mlp", c, 0)]
                for j in range(GUNITS):
                    wait_unit_done(act, c, g, j)
                    if not (last and j >= GUNITS - 2):
                        act.wait_ge(ring_in[(first + j + 2) % 4], g * (16 * GUNITS // 4) + arrivals(first + j + 2))
                        nc.scalar.activation(whi[(first + j) % 2][:, :], wring[(first + j + 2) % 4][:, :], ACT.Copy)\
                            .then_inc(hi_ready, 1)
                    elif c == 0:
                        hi(("wo", 1, 0, j - GUNITS + 2))
                    if j < GT:
                        act.wait_ge(h_lo_ready[c], g * GT + (j + 1))
                        nc.scalar.activation(relu_h[:, j % 2, :], g_bank[(base + j) % 4][:, :], ACT.Relu).then_inc(g_evac, 1)
                        act.wait_ge(g_evac, g * GT + (evacs + j))
                        nc.scalar.activation(hhi[:, j, :], relu_h[:, j % 2, :], ACT.Square).then_inc(h_hi_ready, 1)
                    nh, u = divmod(j - GT, 4)
                    if j >= GT and u == 3 and not (c == 1 and last):
                        for b in range(CB):
                            n = 8 * GROUPS * c + 4 * nh + b
                            act.wait_ge(wide_full, g * 8 + (n + 1))
                            act.wait_ge(y_added, g * 8 + (n + 1))
                            nc.scalar.activation(y_stage[:, b, :], wide[b // 2][:, (b % 2) * 512:(b % 2) * 512 + 512],
                                                 ACT.Copy).then_inc(y_evac, 1)

            def mlp_groups(c):
                act.wait_ge(score_added, 48)
                with act.Fori(0, GROUPS - 1) as g:
                    mlp(c, g, False)
                mlp(c, GROUPS - 1, True)

            act.sem_inc(y_evac, CB)
            copy_out("vecs", vecs[:, :], bank("vecs")[:, 0:37])
            act.wait_ge(g_evac, EV["vecs"])
            hi(units[0])
            transposed(0, "xT", emb_g, emb_b, x_lo_dve, 0)
            hi(units[1])
            copy_out("wuk", wukT[:, :, :], bank("wuk")[:, :].rearrange("p (k c) -> p k c", k=4))
            copy_out("bias", bias_row[:, :], bank("bias")[0:HEADS, 0:FWIN])
            act.wait_ge(g_evac, EV["bias"])
            act.sem_inc(bias_row_ready, 1)
            keys_queries(0)
            products(0)
            for n in range(4):
                copy_out(("near", n), near_bias[:, 2 * n:2 * n + 2, :],
                         bank(("near", n))[:, :].rearrange("p (h n) -> p h n", h=2))
            act.wait_ge(score_added, 16)
            latent_queries(0)
            transposed(1, "xT", emb_g, emb_b, x_lo_pool, 0)
            keys_queries(1)
            products(1)
            attention(0)
            output_projection(0, LN1_0)
            transposed(0, "x1T", l1_g, l1_b, x_lo_dve, KT)
            mlp_groups(0)
            latent_queries(1)
            act.wait_ge(y_added, CB + 8 * GROUPS)
            attention(1)
            output_projection(1, LN1_1)
            transposed(1, "x1T", l1_g, l1_b, x_lo_dve, 2 * KT)
            mlp_groups(1)

        @block.tensor
        def _(pe):
            def free(name):
                if G[name] >= 4:
                    before = uses[G[name] - 4]
                    if before[0] == "proj":
                        pe.wait_ge(wo_added, 8 * before[1] + 4 * before[2] + before[3] + 1)
                    else:
                        pe.wait_ge(g_evac, EV[before])

            def transposes(name, parts):
                free(name)
                ps = bank(name)
                for n, part in enumerate(parts):
                    rows_in_part = part.shape[0]
                    last = nc.tensor.transpose(ps[:, n * P:n * P + rows_in_part] if rows_in_part == P
                                               else ps[:, 0:rows_in_part], part,
                                               ident[0:rows_in_part, 0:rows_in_part])
                last.then_inc(g_full, 1)

            def evacuated(name):
                pe.wait_ge(g_evac, EV[name])

            def x_transposes(c, what):
                if what == "xT":
                    pe.wait_ge(xhat_ready, CB * c + CB)
                else:
                    pe.wait_ge(x1_hat_ready, CB * c + CB)
                for k in range(KT):
                    transposes((what, c, k), [rows[:, b, k * P:(k + 1) * P] for b in range(CB)])

            def x_ready(what, c, k):
                if (what, c) == ("xT", 1):
                    pe.wait_ge(x_lo_pool, k + 1)
                else:
                    pe.wait_ge(x_lo_dve, KT * (0 if what == "xT" else 1 + c) + k + 1)

            def three_passes(out_ap, w_hi, w_lo, m_hi, m_lo, first, last):
                nc.tensor.matmul(out_ap, w_hi, m_hi, start=first, stop=False)
                nc.tensor.matmul(out_ap, w_hi, m_lo, start=False, stop=False)
                return nc.tensor.matmul(out_ap, w_lo, m_hi, start=False, stop=last)

            def column_products(out_ap, slot, x_parts=None):
                h, l = k_columns(whi[slot]), k_columns(wlo[slot])
                m = out_ap.shape[0]
                for k in range(KT):
                    if x_parts:
                        x_ready(*x_parts, k)
                    ins = three_passes(out_ap, h[:, k, 0:m], l[:, k, 0:m], xhi[:, k, :], xlo[:, k, :], k == 0, k == KT - 1)
                return ins

            def project(name, x_parts=None):
                pe.wait_ge(*LO[name])
                free(name)
                m = KEYW if name[0] == "ik" else P
                column_products(bank(name)[0:m, :], U[name] % 2, x_parts).then_inc(g_full, 1)

            def keys_queries(c):
                project(("ik", c), ("xT", c))
                project(("c", c))
                project(("iq", c, 0))
                free(("iw", c))
                evacuated(("ik", c))
                for b in range(CB):
                    last = nc.tensor.transpose(bank(("iw", c))[:, b * HEADS:(b + 1) * HEADS], val[HD:KEYW, 0, b * P:(b + 1) * P],
                                               ident[HD:KEYW, HD:KEYW])
                last.then_inc(g_full, 1)
                evacuated(("c", c))
                transposes(("cR", c), [val[:, 1, b * P:(b + 1) * P] for b in range(CB)])
                for p in (1, 2, 3):
                    project(("iq", c, p))
                latent_transposes(c)

            def latent_transposes(c):
                pe.wait_ge(lat_ready, CB * (c + 1))
                transposes(("cT", c), [lat[:, CB * c + b, :] for b in range(CB)])

            def dot(n):
                i, h = n // HEADS + 2, n % HEADS
                if n in (0, 16):
                    pe.wait_ge(key_lo_ready, n // 16 + 1)
                    pe.wait_ge(iq_lo_ready, 4 * (n // 16) + 4)
                if n >= 2:
                    pe.wait_ge(relu_ready, n - 1)
                length = (i + 1) * P
                q = iq2[:, h, i % CB * P:i % CB * P + P]
                for k0 in range(0, length, 512):
                    k1 = max(min(length, k0 + 512), k0 + 256)
                    nc.tensor.matmul(wide[n % 2][:, k0:k1], q, key_hi[:, k0:k1], start=True, stop=False)
                    last = nc.tensor.matmul(wide[n % 2][:, k0:k1], q, key_lo[:, k0:k1], start=False, stop=True)
                last.then_inc(dots_full, 1)

            def latent_queries(c):
                evacuated(("q", c, 3))
                for h in range(HEADS):
                    name = ("ql", c, h)
                    free(name)
                    half = slice((h % 2) * HD, (h % 2) * HD + HD)
                    nc.tensor.matmul(bank(name)[:, :], wukT[half, h // 2, :], qT[half, h // 2, :],
                                     start=True, stop=True).then_inc(g_full, 1)

            def products(c):
                unit = 0
                for name in tokens_queries(c):
                    if name[0] == "po":
                        g = name[2]
                        pe.wait_ge(pooled_ready, 4 * c + g + 1)
                        free(name)
                        nc.tensor.matmul(bank(name)[:, :], poolw[:, g, :], pooledT[:, g % 2, :],
                                         start=True, stop=True).then_inc(g_full, 1)
                        continue
                    if c == 0:
                        dot(2 * unit)
                        dot(2 * unit + 1)
                    unit += 1
                    project(name)

            def logits(m):
                i, h = divmod(m, HEADS)
                length = (i + 1) * P
                if m >= 2:
                    pe.wait_ge(masked, m - 1)
                for k0 in range(0, length, 512):
                    k1 = min(length, k0 + 512)
                    last = nc.tensor.matmul(wide[m % 2][:, k0:k1], qlatT[:, h, i % CB * P:i % CB * P + P], latT[:, k0:k1],
                                            start=True, stop=True)
                last.then_inc(logits_full, 1)

            def attention(c):
                lo, hi = 32 * c, 32 * c + 32
                evacuated(("ql", c, 7))
                pe.wait_ge(relu_ready, 16 if c == 0 else 48)
                logits(lo)
                logits(lo + 1)
                for step in range(lo, lo + LAST_STEP):
                    for name in attention_step(c, step):
                        if name[0] == "tr":
                            m, t = name[1], name[2]
                            i = m // HEADS
                            pe.wait_ge(exp_ready, m + 1)
                            transposes(name, [logit[:, m % 2, k * P:(k + 1) * P] for k in range(4 * t, min(4 * t + 4, i + 1))])
                        elif name[0] == "pv":
                            v = name[1]
                            i = v // 4
                            m = 2 * v + 1
                            evacuated(("tr", m, (i + 4) // 4 - 1))
                            free(name)
                            for k in range(i + 1):
                                last = nc.tensor.matmul(bank(name)[:, 0:2 * P], lat[:, k, :],
                                                        probsT[:, v % 2, k, :, :].rearrange("p h q -> p (h q)"),
                                                        start=(k == 0), stop=(k == i))
                            last.then_inc(g_full, 1)
                        elif name[0] == "uv":
                            v = name[1]
                            evacuated(("pv", v))
                            free(name)
                            for e in range(2):
                                h = 2 * (v % 4) + e
                                last = nc.tensor.matmul(bank(name)[:, e * HD:e * HD + HD], oT[:, e, :],
                                                        wuv[:, h * HD:h * HD + HD], start=True, stop=True)
                            last.then_inc(g_full, 1)
                        else:
                            i = name[1]
                            pe.wait_ge(att_ready, i + 1)
                            transposes(name, [att[:, i % 2, k * P:(k + 1) * P] for k in range(4)])
                    if step + 2 < hi:
                        logits(step + 2)

            def output_projection(c):
                pe.wait_ge(masked, 32 * c + 32)
                for nh in range(2):
                    for u in range(4):
                        name = ("wo", c, nh, u)
                        pe.wait_ge(*LO[name])
                        slot = U[name] % 2
                        h, l = k_pairs(whi[slot]), k_pairs(wlo[slot])
                        m_hi, m_lo = (pool_hi, pool_lo_part) if u < 2 else (att_hi, att_lo)
                        for b in range(CB):
                            acc = bank(("proj", c, nh, b))[:, :]
                            at = slice(b * P, b * P + P)
                            if u == 0:
                                free(("proj", c, nh, b))
                            for k in range(2):
                                f = 2 * (u % 2) + k
                                if nh == 0 and b == 0:
                                    pe.wait_ge(mix_lo_ready, 8 * c + 2 * u + k + 1)
                                last = three_passes(acc, m_hi[:, f, at], m_lo[:, f, at], h[:, k, :], l[:, k, :],
                                                    u == 0 and k == 0, u == 3 and k == 1)
                            if u == 3:
                                last.then_inc(g_full, 1)
                            elif b == CB - 1:
                                last.then_inc(wo_used, 1)
                            for d in dots_after(c, nh, u, b):
                                dot(d)

            def mlp(c):
                base, evacs = G[("mlp", c, 0)], EV[("mlp", c, 0)]
                sem_lo, lo_base = LO[("mlp", c, 0)]
                split = U[("mlp", c, 0)]
                pe.wait_ge(relu_ready, 48)
                pe.wait_ge(masked, 32 * c + 32)
                with pe.Fori(0, GROUPS) as g:
                    for j in range(GUNITS):
                        pe.wait_ge(sem_lo, g * GUNITS + (lo_base + j))
                        slot = (split + j) % 2
                        if j < GT:
                            pe.wait_ge(g_evac, g * GT + (evacs + j - 4))
                            column_products(g_bank[(base + j) % 4][:, :], slot, ("x1T", c) if j == 0 else None)\
                                .then_inc(g_full, 1)
                            continue
                        nh, u = divmod(j - GT, 4)
                        if nh == 0:
                            pe.wait_ge(h_lo_ready[c], g * GT + (2 * u + 2 + 2))
                        h, l = k_pairs(whi[slot]), k_pairs(wlo[slot])
                        for b in range(CB):
                            if u == 0:
                                pe.wait_ge(y_evac, g * 8 + (8 * GROUPS * c + 4 * nh + b + 1))
                            acc = wide[b // 2][:, (b % 2) * 512:(b % 2) * 512 + 512]
                            at = slice(b * P, b * P + P)
                            for k in range(2):
                                f = 2 * u + k
                                last = three_passes(acc, hhi[:, f, at], hlo[:, f, at], h[:, k, :], l[:, k, :],
                                                    f == 0, f == GT - 1)
                            if u == 3:
                                last.then_inc(wide_full, 1)
                        if u < 3:
                            last.then_inc(unit_used, 1)

            pe.wait_ge(ident_ready, 2)
            pe.wait_ge(small_in, 16 * 6)
            transposes("vecs", [vec_rows[:, :]])
            x_transposes(0, "xT")
            pe.wait_ge(late_in, 16 * 5)
            transposes("wuk", [wuk_raw[:, k * P:(k + 1) * P] for k in range(4)])
            free("bias")
            nc.tensor.matmul(bank("bias")[0:HEADS, 0:FWIN], relb[:, :], hots[:, :], start=True, stop=True).then_inc(g_full, 1)
            keys_queries(0)
            products(0)
            pe.wait_ge(bias_in, 16)
            for n in range(4):
                free(("near", n))
                nc.tensor.matmul(bank(("near", n))[:, :], flip[:, :], near_up[:, 2 * n:2 * n + 2, :].rearrange("p h n -> p (h n)"),
                                 start=True, stop=True).then_inc(g_full, 1)
            latent_queries(0)
            x_transposes(1, "xT")
            keys_queries(1)
            products(1)
            attention(0)
            output_projection(0)
            x_transposes(0, "x1T")
            mlp(0)
            latent_queries(1)
            attention(1)
            output_projection(1)
            x_transposes(1, "x1T")
            mlp(1)


_INS = ["x", "emb_ln_g", "emb_ln_b", "rel_bias", "w_in", "pool_w", "pool_scale", "kv_norm_g", "w_uk", "w_uv", "w_o",
        "ln1_g", "ln1_b", "w_up", "w_down", "ln2_g", "ln2_b"]


def kernel(**inputs):
    import concourse.bacc as bacc
    from concourse.bass_utils import run_bass_kernel_spmd

    nc = bacc.Bacc("TRN2", target_bir_lowering=False, num_devices=1, dynamic_dma_scratch_size=1024)
    arrays, args = {}, []
    for name in _INS:
        a = np.ascontiguousarray(inputs[name])
        arrays[f"in_{name}"] = a
        args.append(nc.dram_tensor(f"in_{name}", a.shape, mybir.dt.from_np(a.dtype), kind="ExternalInput").ap())
    arrays["in_buckets"] = bucket_differences()
    args.append(nc.dram_tensor("in_buckets", (NBUCKET, FWIN), F32, kind="ExternalInput").ap())
    args.append(nc.dram_tensor("normalized_rows", (S, D), F32).ap())
    args.append(nc.dram_tensor("bias_rows", (HEADS, FWIN), F32).ap())
    args.append(nc.dram_tensor("out_0", (1, S, D), F32, kind="ExternalOutput").ap())
    layer(nc, *args)
    r = run_bass_kernel_spmd(nc, [arrays], core_ids=[0])
    return r.results[0]["out_0"]
```

```python
from contextlib import ExitStack

import numpy as np

import concourse.bass as bass
from concourse import mybir

F32 = mybir.dt.float32
F32R = mybir.dt.float32r
ALU = mybir.AluOpType
ACT = mybir.ActivationFunctionType

P = 128
S = 1024
D = 1024
KT = D // P
CHUNK = 512
CB = CHUNK // P
NB = S // P
HEADS = 8
HD = 64
LAT = 128
WINDOWS = (2, 4, 8, 16)
TOPK = 256
FF = 4 * D
NBUCKET = 32
MAX_DIST = 128
ALPHA = 2.0 ** 0.25
EPS = 1e-5
NEG = -1.0e30
TAKEN = -3.0e38
HIST = 16
NEAR = 2 * P
FWIN = NEAR + P

COL_U, COL_Q, COL_C, COL_IQ = 0, 512, 1024, 1152
COL_IK = COL_IQ + HEADS * HD
COL_IW = COL_IK + HD
KEYW = HD + HEADS
GT = 8
GROUPS = FF // P // GT
GUNITS = 2 * GT
KB = 1024


def bucket_differences():
    n = np.maximum(NEAR - 1 - np.arange(FWIN), 0)
    exact = NBUCKET // 2
    large = exact + (np.log(np.maximum(n, 1) / exact) / np.log(MAX_DIST / exact) * exact).astype(np.int64)
    bucket = np.where(n < exact, n, np.minimum(large, NBUCKET - 1))
    hot = (np.arange(NBUCKET)[:, None] == bucket[None, :]).astype(np.float32)
    hot[NBUCKET - 1] -= 1.0
    return hot


def chunk_uses(c):
    uses = [("ik", c), ("c", c)] + (["wuk", "bias"] if c == 0 else []) + [("iq", c, 0), ("iw", c), ("cR", c)] + [("iq", c, p) for p in (1, 2, 3)] + [("cT", c)]
    return uses + tokens_queries(c)


def tokens_queries(c):
    order = ("u0 u1 u2 po0 u3 po1 q0 po2 q1 po3 q2 q3", "q0 q1 q2 u0 u1 u2 po0 u3 po1 q3 po2 po3")[c]
    return [(name[:-1], c, int(name[-1])) for name in order.split()]


def psum_uses():

    def attention(c):
        out = []
        for step in range(32 * c, 32 * c + 32 + 5):
            out += attention_step(c, step)
        return out

    names = ["vecs"] + [("xT", 0, k) for k in range(KT)] + chunk_uses(0)
    names += [("near", n) for n in range(4)] + [("ql", 0, h) for h in range(HEADS)]
    names += [("xT", 1, k) for k in range(KT)] + chunk_uses(1)
    for c in range(2):
        if c:
            names += [("ql", 1, h) for h in range(HEADS)]
        names += attention(c) + [("proj", c, nh, b) for nh in range(2) for b in range(CB)]
        names += [("x1T", c, k) for k in range(KT)] + [("mlp", c, n) for n in range(GROUPS * GT)]
    return names


def attention_step(c, step):
    lo, hi = 32 * c, 32 * c + 32
    out = []
    if step % 2 == 1 and lo <= step - 3 < hi:
        out += [("pv", (step - 3) // 2)]
    uv = [("uv", (step - 4) // 2)] if step % 2 == 0 and lo <= step - 4 < hi else []
    transposes = []
    if step < hi:
        i = step // HEADS
        transposes = [("tr", step, t) for t in range((i + 4) // 4)]
    out += uv + transposes if c else transposes + uv
    if step % HEADS == 4 and lo <= step - 12 < hi:
        out += [("aT", (step - 12) // HEADS)]
    return out


LAST_STEP = 32 + 5


def layer(nc, x, emb_ln_g, emb_ln_b, rel_bias, w_in, pool_w, pool_scale, kv_norm_g, w_uk, w_uv, w_o,
          ln1_g, ln1_b, w_up, w_down, ln2_g, ln2_b, buckets, spill, bias_rows, out):
    uses = psum_uses()
    G = {name: k for k, name in enumerate(uses)}
    TR = {name: n + 1 for n, name in enumerate(name for name in uses if name[0] == "tr")}
    EV = {name: sum(1 for n in uses[:k + 1] if n[0] != "proj") for name, k in G.items()}
    xd = x.rearrange("o (b p) d -> (o b) p d", p=P)
    outd = out.rearrange("o (b p) d -> (o b) p d", p=P)
    spilld = spill.rearrange("(b p) d -> b p d", p=P)
    wind = w_in.rearrange("o (k p) n -> p (o k) n", p=P)
    wod = w_o.rearrange("o (k p) n -> p (o k) n", p=P)
    wupd = w_up.rearrange("o (k p) n -> p (o k) n", p=P)
    wdownd = w_down.rearrange("o (f p) n -> p (o f) n", p=P)

    with ExitStack() as ctx:
        def sb(name, shape, dt=F32):
            return ctx.enter_context(nc.sbuf_tensor(name, shape, dt))

        def sem(name):
            return ctx.enter_context(nc.semaphore(name))

        g_bank = [ctx.enter_context(nc.psum_tensor(f"g_bank{i}", [P, 512], F32)) for i in range(4)]
        wide = [ctx.enter_context(nc.psum_tensor(f"wide{i}", [P, 1024], F32)) for i in range(2)]

        def bank(name):
            return g_bank[G[name] % 4]

        arena_at = -(-nc.sbuf_base // 32) * 32
        sb("arena", [P, (arena_at - nc.sbuf_base + int(104.25 * KB)) // 4])

        def part(name, kb, shape, dt=F32):
            return nc.alloc_sbuf_tensor_at(name, shape, dt, offset=arena_at + int(kb * KB))

        xhi = part("xhi", 0, [P, KT, CHUNK], F32R)
        xlo = part("xlo", 16, [P, KT, CHUNK], F32R)
        probs_hi = [part("probs_hi0", 0, [P, NB, 2, P], F32R), part("probs_hi1", 88.25, [P, NB, 2, P], F32R)]
        probs_lo = [part("probs_lo0", 8, [P, NB, 2, P], F32R), part("probs_lo1", 96.25, [P, NB, 2, P], F32R)]
        logit = part("logit", 16, [P, 2, S])
        mask = part("mask", 24, [P, 2, S])
        qlatT = part("qlatT", 32, [P, HEADS, CHUNK])
        qlat_hi = part("qlat_hi", 32, [P, HEADS, CHUNK], F32R)
        qlat_lo = part("qlat_lo", 48, [P, HEADS, CHUNK], F32R)
        relu_sb = part("relu_sb", 32, [P, 2, S])
        near_up = part("near_up", 40, [P, HEADS, NEAR])
        wuk_raw = part("wuk_raw", 40, [P, HEADS * HD])
        hots = part("hots", 42, [NBUCKET, FWIN])
        bias_row = part("bias_row", 43.5, [HEADS, FWIN])
        vec_rows = part("vec_rows", 45, [37, P])
        hhi = part("hhi", 32, [P, GT, CHUNK], F32R)
        hlo = part("hlo", 48, [P, GT, CHUNK], F32R)
        iq2 = part("iq2", 48, [P, HEADS, CHUNK], F32R)
        att_hi = part("att_hi", 0, [P, 4, CHUNK], F32R)
        att_lo = part("att_lo", 8, [P, 4, CHUNK], F32R)
        pool_hi = part("pool_hi", 16, [P, 4, CHUNK], F32R)
        pool_lo_part = part("pool_lo", 24, [P, 4, CHUNK], F32R)
        att_outT = part("att_outT", 64, [P, 4, CHUNK])
        uT = part("uT", 64, [P, 2, HIST + CHUNK])
        win = part("win", 68.125, [P, 2, HIST + CHUNK])
        pooledT = part("pooledT", 72.25, [P, 2, CHUNK])
        att = part("att", 72, [P, 2, 512])
        oT = part("oT", 76, [P, 2, P])
        relu_h = part("relu_h", 64, [P, 2, CHUNK])
        h_val = part("h_val", 68, [P, 2, CHUNK])
        y_stage = part("y_stage", 72, [P, CB, 512])
        craw = part("craw", 76.25, [P, CB, LAT])
        squares = part("squares", 78.25, [P, CB, LAT])
        lat_val = part("lat_val", 78.25, [P, CB, LAT])
        val = part("val", 80.25, [P, 2, CHUNK])
        latT_hi = part("latT_hi", 80.25, [P, S], F32R)
        work = part("work", 84.25, [P, S])
        latT_lo = part("latT_lo", 84.25, [P, S], F32R)
        pool_out0 = part("pool_out0", 88.25, [P, 4, CHUNK])
        key_hi = part("key_hi", 96.25, [P, S], F32R)
        key_lo = part("key_lo", 100.25, [P, S], F32R)

        rows = sb("rows", [P, CB, D])
        wring = [sb(f"wring{s}", [P, D]) for s in range(4)]
        whi = [sb(f"whi{s}", [P, D], F32R) for s in range(2)]
        wlo = [sb(f"wlo{s}", [P, D], F32R) for s in range(2)]
        score = sb("score", [P, CB, S])
        near_bias = sb("near_bias", [P, HEADS, NEAR])
        qT = sb("qT", [P, 4, CHUNK])
        pool_out = [pool_out0, sb("pool_out1", [P, 4, CHUNK])]
        lat_hi = sb("lat_hi", [P, NB, LAT], F32R)
        lat_lo = sb("lat_lo", [P, NB, LAT], F32R)
        latT = sb("latT", [P, S])
        gains = sb("gains", [P, 2, D])
        ident = sb("ident", [P, P])
        flip = sb("flip", [P, P])
        wukT = sb("wukT", [P, 4, LAT])
        wuv = sb("wuv", [P, HEADS * HD])
        poolw = sb("poolw", [P, 4, P])
        vecs = sb("vecs", [P, 37])
        relb = sb("relb", [NBUCKET, HEADS])
        recip_count = sb("recip_count", [P, HIST])
        count = sb("count", [P, HIST])
        hist = sb("hist", [P, 4, HIST])
        idx_w = sb("idx_w", [P, NB, HEADS])
        stats = sb("stats", [P, CB, 12])
        mean_var = sb("mean_var", [P, 6 * CB, 2])
        rstd = sb("rstd", [P, 6 * CB])
        shift = sb("shift", [P, 6 * CB])
        power = sb("power", [P, 1])
        csum = sb("csum", [P, NB])
        crstd = sb("crstd", [P, NB])
        top8 = sb("top8", [P, 2, 8])
        row_max = sb("row_max", [P, 2])
        neg_max = sb("neg_max", [P, 2])
        exp_sum = sb("exp_sum", [P, 2, HEADS])
        exp_rec = sb("exp_rec", [P, 2, HEADS])

        OUT_SPLIT = {1: slice(0, 512), 2: slice(0, D), 3: slice(0, D)}
        OUT_SHARED = {0: slice(0, D), 1: slice(512, D)}

        def pair_slot(tiles, v):
            return tiles[0][:, CB * (v % 2):CB * (v % 2) + CB, :, :] if v < 16 else tiles[v % 2][:, :, :, :]

        def k_columns(w):
            return w[:, :].rearrange("p (k n) -> p k n", k=KT)

        def k_pairs(w):
            return w[:, :].rearrange("p (k n) -> p k n", k=2)

        emb_g, emb_b, l1_g, l1_b = (vecs[:, 8 * n:8 * n + 8] for n in range(4))
        pscale, kv_g = vecs[:, 32:36], vecs[:, 36:37]

        x_in = [sem(f"x_in{b}") for b in range(NB)]
        small_in = sem("small_in")
        late_in = sem("late_in")
        ring_in = [sem(f"ring_in{s}") for s in range(4)]
        gains_in = sem("gains_in")
        wdown_in = sem("wdown_in")
        rows_in = sem("rows_in")
        spilled = sem("spilled")
        bias_out = sem("bias_out")
        bias_in = sem("bias_in")
        stored = sem("stored")
        g_full = sem("g_full")
        g_evac = sem("g_evac")
        bias_row_ready = sem("bias_row_ready")
        ident_ready = sem("ident_ready")
        const_steps = sem("const_steps")
        counts_ready = sem("counts_ready")
        masks01_ready = sem("masks01_ready")
        dve_steps = sem("dve_steps")
        stats_ready = sem("stats_ready")
        bn_ready = sem("bn_ready")
        var_eps = sem("var_eps")
        rstd_ready = sem("rstd_ready")
        shift_ready = sem("shift_ready")
        xhat_ready = sem("xhat_ready")
        x1_hat_ready = sem("x1_hat_ready")
        emb_rows = sem("emb_rows")
        x1_rows = sem("x1_rows")
        out_rows = sem("out_rows")
        hi_ready = sem("hi_ready")
        lo_dve = sem("lo_dve")
        lo_pool = sem("lo_pool")
        key_lo_ready = sem("key_lo_ready")
        iq_lo_ready = sem("iq_lo_ready")
        mix_hi_ready = sem("mix_hi_ready")
        mix_lo_ready = sem("mix_lo_ready")
        x_lo_dve = sem("x_lo_dve")
        val_ready = sem("val_ready")
        x_lo_pool = sem("x_lo_pool")
        h_ready = sem("h_ready")
        h_lo_ready = [sem(f"h_lo_ready{c}") for c in range(2)]
        unit_used = sem("unit_used")
        wide_full = sem("wide_full")
        y_evac = sem("y_evac")
        csum_ready = sem("csum_ready")
        crstd_ready = sem("crstd_ready")
        lat_ready = sem("lat_ready")
        lat_lo_ready = sem("lat_lo_ready")
        latT_hi_ready = sem("latT_hi_ready")
        latT_lo_ready = sem("latT_lo_ready")
        qlat_lo_ready = sem("qlat_lo_ready")
        probs_lo_ready = sem("probs_lo_ready")
        dots_full = sem("dots_full")
        relu_ready = sem("relu_ready")
        score_added = sem("score_added")
        diag_masked = sem("diag_masked")
        topk_steps = sem("topk_steps")
        topk_turn = sem("topk_turn")
        mask_ready = sem("mask_ready")
        pool_steps = sem("pool_steps")
        pooled_ready = sem("pooled_ready")
        mask_full = sem("mask_full")
        logits_full = sem("logits_full")
        masked = sem("masked")
        neg_max_ready = sem("neg_max_ready")
        exp_ready = sem("exp_ready")
        att_ready = sem("att_ready")
        wo_used = sem("wo_used")
        wo_added = sem("wo_added")
        y_added = sem("y_added")
        last_hat_ready = sem("last_hat_ready")
        last_shared = sem("last_shared")

        units = []
        for c in range(2):
            units += [("ik", c), ("c", c)] + [("iq", c, p) for p in range(4)]
            units += [name for name in tokens_queries(c) if name[0] != "po"]
        for c in range(2):
            units += [("wo", c, nh, u) for nh in range(2) for u in range(4)]
            units += [("mlp", c, j) for j in range(GROUPS * GUNITS)]
        U = {name: n for n, name in enumerate(units)}
        dve_lo = [n for n in units if n in (("ik", 0), ("c", 0), ("iq", 0, 0), ("iq", 0, 1), ("iq", 0, 2), ("iq", 0, 3))
                  or n[:2] == ("mlp", 1)]
        pool_lo = [n for n in units if n not in dve_lo]
        LO = {name: (lo_dve, n + 1) for n, name in enumerate(dve_lo)}
        LO.update({name: (lo_pool, n + 1) for n, name in enumerate(pool_lo)})

        def arrivals(n):
            return 16 * (n // 4 + 1)

        def parts_of(name, w):
            return k_columns(w)[:, :, 0:KEYW] if name[0] == "ik" else w[:, :]

        def wait_unit_done(eng, c, g, j):
            if j < GT:
                eng.wait_ge(g_full, g * GT + (G[("mlp", c, 0)] + j + 1))
                return
            nh, u = divmod(j - GT, 4)
            if u < 3:
                eng.wait_ge(unit_used, g * 6 + (6 * GROUPS * c + 3 * nh + u + 1))
            else:
                eng.wait_ge(wide_full, g * 8 + (8 * GROUPS * c + 4 * nh + 4))

        def wait_product(eng, name):
            if name[0] == "mlp":
                wait_unit_done(eng, name[1], name[2] // GUNITS, name[2] % GUNITS)
            elif name[0] != "wo":
                eng.wait_ge(g_full, G[name] + 1)
            elif name[3] == 3:
                eng.wait_ge(g_full, G[("proj", name[1], name[2], CB - 1)] + 1)
            else:
                eng.wait_ge(wo_used, 6 * name[1] + 3 * name[2] + name[3] + 1)

        def split_lo(eng, name, sem_lo, at=None):
            n = U[name]
            eng.wait_ge(hi_ready, n + 1 if at is None else at)
            eng.tensor_tensor(parts_of(name, wlo[n % 2]), parts_of(name, wring[n % 4]),
                              parts_of(name, whi[n % 2]).bitcast(F32), ALU.subtract).then_inc(sem_lo, 1)

        EMB0, EMB1, LN1_0, LN2_0, LN1_1, LN2_1 = range(6)
        LN2_STEP = 46

        block = ctx.enter_context(nc.Block())

        @block.sync
        def _(sp):
            def load_unit(name):
                n = U[name]
                slot = wring[n % 4]
                if n >= 4:
                    sp.wait_ge(*LO[units[n - 4]])
                if name[0] == "wo":
                    _, c, nh, u = name
                    sp.dma_start(k_pairs(slot), wod[:, 2 * u:2 * u + 2, nh * 512:nh * 512 + 512]).then_inc(ring_in[n % 4], 16)
                elif name[0] == "ik":
                    sp.dma_start(parts_of(name, slot), wind[:, :, COL_IK:COL_IK + KEYW]).then_inc(ring_in[n % 4], 16)
                else:
                    col = {"c": COL_C, "iq": COL_IQ, "q": COL_Q, "u": COL_U}[name[0]] + (P * name[2] if name[0] != "c" else 0)
                    sp.dma_start(k_columns(slot), wind[:, :, col:col + P]).then_inc(ring_in[n % 4], 16)

            def load_gains(g, b):
                sp.dma_start(gains[:, 0, :], g.to_broadcast([P, D])).then_inc(gains_in, 16)
                sp.dma_start(gains[:, 1, :], b.to_broadcast([P, D])).then_inc(gains_in, 16)

            def load_mlp(c):
                first = U[("mlp", c, 0)]
                sem_lo, lo_base = LO[("mlp", c, 0)]
                sp.wait_ge(*LO[units[first - 1]])
                with sp.Fori(0, GROUPS) as g:
                    for j in range(GUNITS):
                        slot = (first + j) % 4
                        sp.wait_ge(sem_lo, g * GUNITS + (lo_base - 1 + j - 4 + 1))
                        if j < GT:
                            src = wupd[:, :, bass.ds(g * (GT * P) + j * P, P)]
                            dst = k_columns(wring[slot])
                        else:
                            nh, u = divmod(j - GT, 4)
                            src = wdownd[:, bass.ds(g * GT + 2 * u, 2), nh * 512:nh * 512 + 512]
                            dst = k_pairs(wring[slot])
                        sp.dma_start(dst, src).then_inc(ring_in[slot], 16)

            def store():
                for b in range(CB):
                    sp.wait_ge(out_rows, b + 1)
                    sp.dma_start(outd[b], rows[:, b, :]).then_inc(stored, 16)

            def load_units(names):
                for name in names:
                    load_unit(name)

            for b in range(CB):
                sp.dma_start(rows[:, b, :], xd[b]).then_inc(x_in[b], 16)
            sp.dma_start(vec_rows[0:8, :], emb_ln_g.rearrange("(k p) -> k p", p=P)).then_inc(small_in, 16)
            sp.dma_start(vec_rows[8:16, :], emb_ln_b.rearrange("(k p) -> k p", p=P)).then_inc(small_in, 16)
            sp.dma_start(vec_rows[16:24, :], ln1_g.rearrange("o (k p) -> (o k) p", p=P)).then_inc(small_in, 16)
            sp.dma_start(vec_rows[24:32, :], ln1_b.rearrange("o (k p) -> (o k) p", p=P)).then_inc(small_in, 16)
            sp.dma_start(vec_rows[32:36, :], pool_scale.rearrange("o (k p) -> (o k) p", p=P)).then_inc(small_in, 16)
            sp.dma_start(vec_rows[36:37, :], kv_norm_g).then_inc(small_in, 16)
            load_unit(units[0])
            load_unit(units[1])
            load_unit(units[2])
            load_unit(units[3])
            sp.dma_start(wuk_raw[:, :], w_uk.rearrange("o c h d -> (o c) (h d)")).then_inc(late_in, 16)
            sp.dma_start(relb[:, :], rel_bias).then_inc(late_in, 16)
            sp.dma_start(hots[:, :], buckets).then_inc(late_in, 16)
            sp.dma_start(wuv[:, :], w_uv.rearrange("o c h d -> (o c) (h d)")).then_inc(late_in, 16)
            sp.dma_start(poolw[:, :, :], pool_w.rearrange("o g c d -> c (o g) d")).then_inc(late_in, 16)
            load_gains(emb_ln_g.rearrange("(o d) -> o d", o=1), emb_ln_b.rearrange("(o d) -> o d", o=1))
            load_units(units[4:7])
            for b in range(CB):
                sp.wait_ge(emb_rows, b + 1)
                sp.dma_start(spilld[b], rows[:, b, :]).then_inc(spilled, 16)
            sp.wait_ge(spilled, 16 * CB)
            for b in range(CB):
                sp.dma_start(rows[:, b, :], xd[CB + b]).then_inc(x_in[CB + b], 16)
            sp.wait_ge(bias_row_ready, 1)
            sp.dma_start(bias_rows, bias_row[:, :]).then_inc(bias_out, 16)
            sp.wait_ge(bias_out, 16)
            sp.dma_start(near_up[:, :, :], bass.AP(tensor=bias_rows.tensor, offset=0, ap=[[1, P], [FWIN, HEADS], [1, NEAR]])
                         ).then_inc(bias_in, 16)
            load_units(units[7:U[("wo", 0, 1, 0)]])
            for b in range(CB):
                sp.wait_ge(emb_rows, CB + b + 1)
                sp.dma_start(spilld[CB + b], rows[:, b, :]).then_inc(spilled, 16)
            load_gains(ln1_g, ln1_b)
            sp.wait_ge(spilled, 16 * NB)
            for b in range(CB):
                sp.dma_start(rows[:, b, :], spilld[b]).then_inc(rows_in, 16)
            load_units(units[U[("wo", 0, 1, 0)]:U[("mlp", 0, 0)]])
            load_mlp(0)
            load_units(units[U[("wo", 1, 0, 0)]:U[("wo", 1, 1, 0)]])
            sp.wait_ge(x1_rows, CB)
            load_gains(ln2_g, ln2_b)
            store()
            load_gains(ln1_g, ln1_b)
            sp.wait_ge(stored, 16 * CB)
            for b in range(CB):
                sp.dma_start(rows[:, b, :], spilld[CB + b]).then_inc(rows_in, 16)
            load_units(units[U[("wo", 1, 1, 0)]:U[("mlp", 1, 0)]])
            load_mlp(1)
            sp.wait_ge(x1_rows, 2 * CB)
            load_gains(ln2_g, ln2_b)
            for b, at, done, count in ((0, slice(0, D), last_shared, 2), (2, slice(0, D), out_rows, CB + 2),
                                       (3, slice(0, 512), out_rows, CB + 3), (3, slice(512, D), out_rows, CB + 4),
                                       (1, slice(0, D), last_shared, 4)):
                sp.wait_ge(done, count)
                sp.dma_start(outd[CB + b][:, at], rows[:, b, at]).then_inc(stored, 16)
            sp.wait_ge(stored, 16 * (NB + 1))

        def pooling(eng, c, link):
            for g, w in enumerate(WINDOWS):
                u = uT[:, g % 2, :]
                eng.wait_ge(g_evac, EV[("u", c, g)])
                link(eng.tensor_copy(u[:, 0:HIST], hist[:, g, :]))
                src, reach = u, 1
                while reach < w:
                    dst = win[:, (reach.bit_length() - 1) % 2, :]
                    link(eng.tensor_tensor(dst[:, reach:HIST + CHUNK], src[:, reach:HIST + CHUNK],
                                           src[:, 0:HIST + CHUNK - reach], ALU.add))
                    src, low, reach = dst, reach, 2 * reach
                    if reach < w:
                        link(eng.tensor_copy(dst[:, 0:low], u[:, 0:low]))
                done = pooledT[:, g % 2, :]
                if g >= 2:
                    eng.wait_ge(g_full, G[("po", c, g - 2)] + 1)
                link(eng.tensor_scalar(done, src[:, HIST:HIST + CHUNK], 1.0 / w, None, ALU.mult))
                if c == 0:
                    link(eng.tensor_tensor(done[:, 0:w - 1], src[:, HIST:HIST + w - 1], recip_count[:, 0:w - 1], ALU.mult))
                    link(eng.tensor_copy(hist[:, g, :], u[:, CHUNK:CHUNK + HIST]))
                eng.tensor_tensor(done, done, u[:, HIST:HIST + CHUNK], ALU.subtract).then_inc(pooled_ready, 1)
                yield g

        def x_lo(eng, what, c, sem_lo, affine=None):
            for k in range(KT):
                if affine and k % 2:
                    gain, bias = affine
                    eng.wait_ge(g_evac, EV[(what, c, k)])
                    eng.tensor_scalar(val[:, k % 2, :], bank((what, c, k))[:, :], gain[:, k:k + 1], bias[:, k:k + 1],
                                      ALU.mult, ALU.add).then_inc(val_ready, 1)
                    eng.wait_ge(val_ready, (0 if what == "xT" else 4 + 4 * c) + k // 2 + 1)
                eng.wait_ge(g_evac, EV[(what, c, k)])
                eng.tensor_tensor(xlo[:, k, :], val[:, k % 2, :], xhi[:, k, :].bitcast(F32), ALU.subtract).then_inc(sem_lo, 1)

        def projection_steps():
            return [(nh, u, b) for nh in range(2) for u in range(4) for b in range(CB)]

        LAST_DOTS = (46, 47)

        def dots_after(c, nh, u, b):
            n = 16 * nh + 4 * u + b
            doubled = (6, 14, 22)
            if c or n > 26:
                return []
            first = 16 + n + sum(1 for d in doubled if d < n)
            return [first, first + 1] if n in doubled else [first]

        def keys_queries_lo(eng, c, link, between=None):
            eng.wait_ge(g_evac, EV[("ik", c)])
            at = slice(c * CHUNK, (c + 1) * CHUNK)
            link(eng.tensor_tensor(key_lo[0:HD, at], val[0:HD, 0, :], key_hi[0:HD, at].bitcast(F32), ALU.subtract))
            eng.tensor_tensor(key_lo[HD:P, at], val[0:HD, 0, :], key_hi[0:HD, at].bitcast(F32), ALU.subtract)                .then_inc(key_lo_ready, 1)
            eng.wait_ge(key_lo_ready, c + 1)
            for p in range(4):
                if between:
                    between(p)
                eng.wait_ge(g_evac, EV[("iq", c, p)])
                parts = []
                for e in range(2):
                    hi_half, lo_half = slice(e * HD, e * HD + HD), slice(HD - e * HD, 2 * HD - e * HD)
                    parts.append((iq2[lo_half, 2 * p + e, :], val[hi_half, p % 2, :], iq2[hi_half, 2 * p + e, :].bitcast(F32)))
                link(eng.tensor_tensor(*parts[0], ALU.subtract))
                eng.tensor_tensor(*parts[1], ALU.subtract).then_inc(iq_lo_ready, 1)
                eng.wait_ge(iq_lo_ready, 4 * c + p + 1)
                if p == 2:
                    eng.wait_ge(lat_ready, CB * c + CB)
                    eng.tensor_tensor(lat_lo[:, CB * c:CB * c + CB, :], lat_val[:, :, :],
                                      lat_hi[:, CB * c:CB * c + CB, :].bitcast(F32), ALU.subtract).then_inc(lat_lo_ready, 1)
                    eng.wait_ge(lat_lo_ready, c + 1)

        def mlp_lo(eng, c, g, last, before=None):
            sem_lo = LO[("mlp", c, 0)][0]
            for j in range(GUNITS):
                if before:
                    before(j)
                if not (last and j >= GUNITS - 2):
                    split_lo(eng, ("mlp", c, (j + 2) % GUNITS), sem_lo, g * GUNITS + (U[("mlp", c, 0)] + j + 3))
                if j < GT:
                    eng.wait_ge(h_ready, g * GT + (GT * GROUPS * c + j + 1))
                    eng.tensor_tensor(hlo[:, j, :], h_val[:, j % 2, :], hhi[:, j, :].bitcast(F32), ALU.subtract)\
                        .then_inc(h_lo_ready[c], 1)

        def emb_gains(eng, c, link):
            eng.wait_ge(gains_in, 32)
            eng.wait_ge(g_full, G[("xT", c, KT - 1)] + 1)
            for b in range(CB):
                link(eng.tensor_tensor(rows[:, b, :], rows[:, b, :], gains[:, 0, :], ALU.mult))
                eng.tensor_tensor(rows[:, b, :], rows[:, b, :], gains[:, 1, :], ALU.add).then_inc(emb_rows, 1)
                yield b

        def x1_gains(eng, c, link):
            eng.wait_ge(gains_in, 32 * (2 if c == 0 else 4))
            for n in range(2):
                link(eng.tensor_scalar(gains[:, n, :], gains[:, n, :], ALPHA, None, ALU.mult))
            eng.wait_ge(g_full, G[("x1T", c, KT - 1)] + 1)
            for b in range(CB):
                link(eng.tensor_tensor(rows[:, b, :], rows[:, b, :], gains[:, 0, :], ALU.mult))
                eng.tensor_tensor(rows[:, b, :], rows[:, b, :], gains[:, 1, :], ALU.add).then_inc(x1_rows, 1)

        @block.gpsimd
        def _(pool):
            pool.memset(ident[:, :], 0.0).then_inc(const_steps, 1)
            pool.wait_ge(const_steps, 1)
            pool.affine_select(out=ident[:, :], in_=ident[:, :], compare_op=ALU.not_equal, fill=1.0, base=0,
                               pattern=[[-1, P]], channel_multiplier=1).then_inc(ident_ready, 1)
            pool.memset(flip[:, :], 0.0).then_inc(const_steps, 1)
            pool.wait_ge(const_steps, 2)
            pool.affine_select(out=flip[:, :], in_=flip[:, :], compare_op=ALU.not_equal, fill=1.0, base=1 - P,
                               pattern=[[1, P]], channel_multiplier=1).then_inc(ident_ready, 1)
            pool.memset(power[:, :], -0.5).then_inc(const_steps, 1)
            pool.sem_inc(y_added, CB)
            pool.sem_inc(h_lo_ready[0], 2)
            pool.iota(count[:, :], pattern=[[1, HIST]], base=1, channel_multiplier=0,
                      allow_small_or_imprecise_dtypes=True).then_inc(counts_ready, 1)
            pool.memset(hist[:, :, :], 0.0).then_inc(const_steps, 1)
            for i in range(2):
                pool.memset(score[:, i, 0:CHUNK], 0.0).then_inc(const_steps, 1)
            pool.wait_ge(const_steps, 6)
            for i in range(2):
                diag = score[:, i, i * P:(i + 1) * P]
                pool.affine_select(out=diag, in_=diag, compare_op=ALU.is_ge, fill=NEG, base=0,
                                   pattern=[[-1, P]], channel_multiplier=1).then_inc(masks01_ready, 1)

            steps = [0]

            def link(ins):
                steps[0] += 1
                ins.then_inc(pool_steps, 1)
                pool.wait_ge(pool_steps, steps[0])

            def inverse_std(l, blocks=range(CB)):
                for b in blocks:
                    n = 4 * l + b
                    pool.wait_ge(stats_ready, n + 1)
                    pool.tensor_scalar(rstd[:, n:n + 1], mean_var[:, n, 1:2], EPS, None, ALU.add).then_inc(var_eps, 1)
                    pool.wait_ge(var_eps, n + 1)
                    pool.tensor_tensor(rstd[:, n:n + 1], rstd[:, n:n + 1], power[:, :], ALU.pow).then_inc(rstd_ready, 1)
                    if l in (LN1_0, LN1_1) or (l == LN2_1 and b in OUT_SHARED):
                        pool.wait_ge(rstd_ready, n + 1)
                        pool.tensor_scalar(shift[:, n:n + 1], mean_var[:, n, 0:1], rstd[:, n:n + 1], -1.0, ALU.mult, ALU.mult)\
                            .then_inc(shift_ready, 1)

            def latents_inverse_rms(c):
                at = slice(CB * c, CB * c + CB)
                pool.wait_ge(csum_ready, CB * c + CB)
                link(pool.tensor_scalar(crstd[:, at], csum[:, at], 1.0 / LAT, EPS, ALU.mult, ALU.add))
                pool.tensor_tensor(crstd[:, at], crstd[:, at], power[:, :].to_broadcast([P, CB]), ALU.pow)\
                    .then_inc(crstd_ready, 1)

            def diagonals(blocks):
                for i in blocks:
                    pool.wait_ge(score_added, 8 * (i - 2) + 8)
                    diag = score[:, i % CB, i * P:(i + 1) * P]
                    pool.affine_select(out=diag, in_=diag, compare_op=ALU.is_ge, fill=TAKEN, base=0,
                                       pattern=[[-1, P]], channel_multiplier=1).then_inc(diag_masked, 1)

            def head_masks(c):
                pool.wait_ge(g_full, G[("po", 1, 3)] + 1)
                for m in range(32 * c, 32 * c + 32):
                    i, h = divmod(m, HEADS)
                    length = (i + 1) * P
                    near = min(NEAR, length)
                    if h == 0 and i >= 2:
                        pool.wait_ge(mask_ready, i - 1)
                    if c == 1 and m in range(LN2_STEP + 3, LN2_STEP + 15, 3):
                        inverse_std(LN2_0, [(m - LN2_STEP) // 3 - 1])
                    if m >= 2:
                        pool.wait_ge(masked, m - 1)
                    if h < 2 and length > NEAR:
                        pool.tensor_copy(mask[:, m % 2, 0:length - NEAR], score[:, i % CB, 0:length - NEAR])
                    pool.tensor_tensor(mask[:, m % 2, length - near:length], score[:, i % CB, length - near:length],
                                       near_bias[:, h, NEAR - near:NEAR], ALU.add).then_inc(mask_full, 1)

            def add_y(c, g, nh):
                pool.wait_ge(x1_rows, CB * c + CB)
                for b in range(CB):
                    pool.wait_ge(y_evac, g * 8 + (8 * GROUPS * c + 4 * nh + b + 1 + CB))
                    piece = rows[:, b, nh * 512:nh * 512 + 512]
                    pool.tensor_tensor(piece, piece, y_stage[:, b, :], ALU.add).then_inc(y_added, 1)

            def lo(*names):
                for name in names:
                    split_lo(pool, name, lo_pool)

            inverse_std(EMB0)
            for b in emb_gains(pool, 0, link):
                pass
            latents_inverse_rms(0)
            lo(*units[U[("u", 0, 0)]:U[("q", 0, 2)]])
            inverse_std(EMB1, [0])
            lo(("q", 0, 2))
            inverse_std(EMB1, [1])
            lo(("q", 0, 3))
            inverse_std(EMB1, [2, 3])
            diagonals((2, 3))
            lo(("ik", 1), ("c", 1))
            x_lo(pool, "xT", 1, x_lo_pool)
            lo(("iq", 1, 0), ("iq", 1, 1))

            def ahead(p):
                if p == 1:
                    latents_inverse_rms(1)
                unit = units[U[("iq", 1, p)] + 2]
                lo(unit)
                pool.wait_ge(*LO[unit])

            pool.wait_ge(*LO[("iq", 1, 1)])
            keys_queries_lo(pool, 1, link, ahead)
            lo(*units[U[("iq", 1, 3)] + 3:U[("wo", 0, 0, 2)]])
            head_masks(0)
            lo(*units[U[("wo", 0, 0, 2)]:U[("mlp", 0, 0)]])
            inverse_std(LN1_0)
            lo(("mlp", 0, 0), ("mlp", 0, 1))
            diagonals((4, 5, 6, 7))

            def add_at(c, g):
                def before(j):
                    if j in (GT + 3, GT + 7):
                        add_y(c, g, (j - GT) // 4)
                return before

            with pool.Fori(0, GROUPS - 1) as g:
                mlp_lo(pool, 0, g, False, add_at(0, g))
            mlp_lo(pool, 0, GROUPS - 1, True, add_at(0, GROUPS - 1))
            lo(("wo", 1, 0, 0), ("wo", 1, 0, 1))
            head_masks(1)
            lo(*units[U[("wo", 1, 0, 2)]:U[("mlp", 1, 0)]])
            inverse_std(LN1_1)
            x1_gains(pool, 1, link)
            pool.wait_ge(x1_rows, NB)
            with pool.Fori(0, GROUPS - 1) as g:
                add_y(1, g, 0)
                add_y(1, g, 1)
            inverse_std(LN2_1, [0, 1])
            pool.wait_ge(gains_in, 32 * 5)
            for b, at in OUT_SHARED.items():
                pool.wait_ge(last_hat_ready, b + 1)
                for n, op in enumerate((ALU.mult, ALU.add)):
                    y = rows[:, b, at]
                    pool.tensor_tensor(y, y, gains[:, n, at], op).then_inc(last_shared, 1)
                    if b == 0:
                        inverse_std(LN2_1, [2 + n])
                    pool.wait_ge(last_shared, 2 * b + n + 1)

        @block.vector
        def _(dve):
            n_steps = [0]

            def chain(ins):
                n_steps[0] += 1
                ins.then_inc(dve_steps, 1)
                dve.wait_ge(dve_steps, n_steps[0])

            def statistics(l, b):
                nc.vector.bn_stats(stats[:, b, 0:6], rows[:, b, 0:512])
                chain(nc.vector.bn_stats(stats[:, b, 6:12], rows[:, b, 512:1024]))
                nc.vector.bn_aggr(mean_var[:, 4 * l + b, :], stats[:, b, :]).then_inc(stats_ready, 1)

            def normalize(l, c):
                for b in range(CB + 1):
                    if b < CB:
                        dve.wait_ge(x_in[CB * c + b], 16)
                        statistics(l, b)
                    if b > 0:
                        n = 4 * l + b - 1
                        dve.wait_ge(rstd_ready, n + 1)
                        nc.vector.tensor_scalar(rows[:, b - 1, :], rows[:, b - 1, :], mean_var[:, n, 0:1], rstd[:, n:n + 1],
                                                ALU.subtract, ALU.mult).then_inc(xhat_ready, 1)
                    yield b

            def out_norm_first(c, l, b, at=slice(0, D)):
                dve.wait_ge(gains_in, 32 * (3 if c == 0 else 5))
                dve.wait_ge(stats_ready, 4 * l + b + 1)
                y = rows[:, b, at]
                chain(nc.vector.scalar_tensor_tensor(out=y, in0=y, scalar=mean_var[:, 4 * l + b, 0:1], in1=gains[:, 0, at],
                                                     op0=ALU.subtract, op1=ALU.mult))

            def out_norm_second(l, b, at=slice(0, D)):
                n = 4 * l + b
                y = rows[:, b, at]
                dve.wait_ge(rstd_ready, n + 1)
                nc.vector.scalar_tensor_tensor(out=y, in0=y, scalar=rstd[:, n:n + 1], in1=gains[:, 1, at],
                                               op0=ALU.mult, op1=ALU.add).then_inc(out_rows, 1)

            def add_score(n):
                i, h = n // HEADS + 2, n % HEADS
                length = (i + 1) * P
                s = score[:, i % CB, 0:length]
                if n == 16:
                    dve.wait_ge(mask_full, 32)
                dve.wait_ge(relu_ready, n + 1)
                if h == 0:
                    nc.vector.tensor_scalar(s, relu_sb[:, n % 2, 0:length], idx_w[:, i, h:h + 1], None, ALU.mult)\
                        .then_inc(score_added, 1)
                else:
                    dve.wait_ge(score_added, n)
                    nc.vector.scalar_tensor_tensor(out=s, in0=relu_sb[:, n % 2, 0:length],
                                                   scalar=idx_w[:, i, h:h + 1], in1=s, op0=ALU.mult, op1=ALU.add)\
                        .then_inc(score_added, 1)

            def mask_of(i, w):
                s = score[:, i % CB, 0:(i + 1) * P]
                chain(nc.vector.tensor_tensor(s, w, s, ALU.is_equal))
                nc.vector.tensor_scalar(s, s, NEG, None, ALU.mult).then_inc(mask_ready, 1)

            def select_pair():
                w = [work[:, 0:3 * P], work[:, 3 * P:7 * P]]
                dve.wait_ge(diag_masked, 2)
                for e in range(2):
                    nc.vector.tensor_copy(w[e], score[:, 2 + e, 0:(3 + e) * P]).then_inc(topk_steps, 1)
                with dve.Fori(0, TOPK // 8) as r:
                    for e in range(2):
                        dve.wait_ge(topk_steps, 4 * r + (1 + e))
                        dve.sem_inc(topk_turn, 1)
                        nc.vector.max(top8[:, e, :], w[e]).then_inc(topk_steps, 1)
                    for e in range(2):
                        dve.wait_ge(topk_steps, 4 * r + (3 + e))
                        dve.sem_inc(topk_turn, 1)
                        nc.vector.match_replace(w[e], top8[:, e, :], w[e], TAKEN).then_inc(topk_steps, 1)
                dve.wait_ge(topk_steps, 2 + 4 * (TOPK // 8))
                for e in range(2):
                    mask_of(2 + e, w[e])

            def select(i):
                length = (i + 1) * P
                s = score[:, i % CB, 0:length]
                w = work[:, 0:length]
                rounds = TOPK // 8
                first = 2 + 4 * rounds + (2 * rounds + 1) * (i - 4)
                dve.wait_ge(diag_masked, i - 1)
                nc.vector.tensor_copy(w, s).then_inc(topk_steps, 1)
                with dve.Fori(0, rounds) as r:
                    dve.wait_ge(topk_steps, 2 * r + (first + 1))
                    dve.sem_inc(topk_turn, 1)
                    nc.vector.max(top8[:, 0, :], w).then_inc(topk_steps, 1)
                    dve.wait_ge(topk_steps, 2 * r + (first + 2))
                    dve.sem_inc(topk_turn, 1)
                    nc.vector.match_replace(w, top8[:, 0, :], w, TAKEN).then_inc(topk_steps, 1)
                dve.wait_ge(topk_steps, first + 2 * rounds + 1)
                mask_of(i, w)

            def mask_logits(m):
                i, h = divmod(m, HEADS)
                length = (i + 1) * P
                dve.wait_ge(logits_full, m + 1)
                dve.wait_ge(mask_full, m + 1)
                if m >= 2:
                    i2 = (m - 2) // HEADS
                    dve.wait_ge(g_full, G[("tr", m - 2, (i2 + 4) // 4 - 1)] + 1)
                nc.vector.tensor_tensor_reduce(logit[:, m % 2, 0:length], wide[m % 2][:, 0:length],
                                               mask[:, m % 2, 0:length], 1.0, TAKEN, ALU.add, ALU.max,
                                               row_max[:, m % 2:m % 2 + 1]).then_inc(masked, 1)
                dve.wait_ge(masked, m + 1)
                nc.vector.tensor_scalar(neg_max[:, m % 2:m % 2 + 1], row_max[:, m % 2:m % 2 + 1], -1.0, None,
                                        ALU.mult).then_inc(neg_max_ready, 1)

            def probabilities_lo(m):
                i = m // HEADS
                for t in range((i + 4) // 4):
                    name = ("tr", m, t)
                    n = min(4, i + 1 - 4 * t)
                    at = slice(4 * t, 4 * t + n)
                    dve.wait_ge(g_evac, EV[name])
                    nc.vector.tensor_tensor(pair_slot(probs_lo, m // 2)[:, at, m % 2, :],
                                            bank(name)[:, 0:n * P].rearrange("p (k q) -> p k q", k=n),
                                            pair_slot(probs_hi, m // 2)[:, at, m % 2, :].bitcast(F32),
                                            ALU.subtract).then_inc(probs_lo_ready, 1)

            def latent_parts_lo():
                dve.wait_ge(latT_hi_ready, 1)
                nc.vector.tensor_tensor(latT_lo[:, :], latT[:, :], latT_hi[:, :].bitcast(F32), ALU.subtract)\
                    .then_inc(latT_lo_ready, 1)
                for h in range(HEADS):
                    name = ("ql", 1, h)
                    dve.wait_ge(g_evac, EV[name])
                    nc.vector.scalar_tensor_tensor(out=qlat_lo[:, h, :], in0=bank(name)[:, :], scalar=HD ** -0.5,
                                                   in1=qlat_hi[:, h, :].bitcast(F32), op0=ALU.mult, op1=ALU.subtract)\
                        .then_inc(qlat_lo_ready, 1)

            def scale_heads(i):
                dve.wait_ge(exp_ready, 8 * i + 8)
                chain(nc.vector.reciprocal(exp_rec[:, i % 2, :], exp_sum[:, i % 2, :]))
                dve.wait_ge(g_evac, EV[("uv", 4 * i + 3)])
                a = att[:, i % 2, :].rearrange("p (h d) -> p h d", h=HEADS)
                nc.vector.tensor_tensor(a, a, exp_rec[:, i % 2, :].unsqueeze(2).to_broadcast([P, HEADS, HD]), ALU.mult)\
                    .then_inc(att_ready, 1)

            def attention(c):
                for step in range(32 * c, 32 * c + 32 + 5):
                    if step < 32 * c + 32:
                        mask_logits(step)
                    if step == 16:
                        next(gained)
                    if 32 * c + 2 <= step < 32 * c + 34:
                        probabilities_lo(step - 2)
                    if step % HEADS == 3 and step - 11 >= 32 * c:
                        scale_heads((step - 11) // HEADS)
                    b, piece = divmod(step - LN2_STEP, 3)
                    if c == 1 and 0 <= b < CB:
                        n = 4 * LN2_0 + b
                        if piece == 0:
                            dve.wait_ge(y_added, CB + 8 * GROUPS - 4 + b + 1)
                            statistics(LN2_0, b)
                        elif piece == 1:
                            out_norm_first(0, LN2_0, b)
                        else:
                            out_norm_second(LN2_0, b)
                    if step == 32 * c + 34:
                        mix_lo(c, 0)

            def mix_lo(c, n):
                raw, hi_part, lo_part = ((pool_out[c], pool_hi, pool_lo_part), (att_outT, att_hi, att_lo))[n]
                for k in range(4):
                    dve.wait_ge(mix_hi_ready, 8 * c + 4 * n + k + 1)
                    nc.vector.tensor_tensor(lo_part[:, k, :], raw[:, k, :], hi_part[:, k, :].bitcast(F32), ALU.subtract)\
                        .then_inc(mix_lo_ready, 1)

            def add_residual(c, l):
                dve.wait_ge(rows_in, 16 * CB * (c + 1))
                for nh, u, b in projection_steps():
                    n = 8 * c + 4 * nh + b
                    if u == 3:
                        dve.wait_ge(g_full, G[("proj", c, nh, b)] + 1)
                        piece = rows[:, b, nh * 512:nh * 512 + 512]
                        nc.vector.scalar_tensor_tensor(out=piece, in0=piece, scalar=ALPHA, in1=bank(("proj", c, nh, b))[:, :],
                                                       op0=ALU.mult, op1=ALU.add).then_inc(wo_added, 1)
                        dve.wait_ge(wo_added, n + 1)
                        nc.vector.bn_stats(stats[:, b, 6 * nh:6 * nh + 6], piece).then_inc(bn_ready, 1)
                        if nh == 1:
                            dve.wait_ge(bn_ready, n + 1)
                            nc.vector.bn_aggr(mean_var[:, 4 * l + b, :], stats[:, b, :]).then_inc(stats_ready, 1)
                    for d in dots_after(c, nh, u, b):
                        add_score(d)

            def last_products():
                for b in range(CB):
                    dve.wait_ge(wide_full, 16 * GROUPS - 4 + b + 1)
                    add_last(1, b)
                    half_statistics(1, b)
                    nc.vector.bn_aggr(mean_var[:, 4 * LN2_1 + b, :], stats[:, b, :]).then_inc(stats_ready, 1)
                    if b > 1:
                        out_norm_second(LN2_1, b - 1, OUT_SPLIT[b - 1])
                    if b > 0:
                        out_norm_first(1, LN2_1, b, OUT_SPLIT[b])
                for half in range(2):
                    out_norm_second(LN2_1, CB - 1, slice(512 * half, 512 * half + 512))

            def half_statistics(nh, b):
                dve.wait_ge(y_evac, CB + 16 * GROUPS - 8 + 4 * nh + b + 1)
                chain(nc.vector.bn_stats(stats[:, b, 6 * nh:6 * nh + 6], rows[:, b, nh * 512:nh * 512 + 512]))

            def add_last(nh, b):
                piece = rows[:, b, nh * 512:nh * 512 + 512]
                nc.vector.tensor_tensor(piece, piece, wide[b // 2][:, (b % 2) * 512:(b % 2) * 512 + 512], ALU.add)\
                    .then_inc(y_evac, 1)

            def first_half(j):
                if j == GT + 3:
                    dve.wait_ge(y_added, CB + 16 * GROUPS - 8)
                    for b in range(CB):
                        dve.wait_ge(wide_full, 16 * GROUPS - 8 + b + 1)
                        add_last(0, b)
                        half_statistics(0, b)

            dve.sem_inc(h_lo_ready[1], 2)
            dve.wait_ge(counts_ready, 1)
            nc.vector.reciprocal(recip_count[:, :], count[:, :]).then_inc(counts_ready, 1)
            for step in normalize(EMB0, 0):
                pass
            split_lo(dve, ("ik", 0), lo_dve)
            x_lo(dve, "xT", 0, x_lo_dve, (emb_g, emb_b))
            split_lo(dve, ("c", 0), lo_dve)
            split_lo(dve, ("iq", 0, 0), lo_dve)
            keys_queries_lo(dve, 0, chain, lambda p: split_lo(dve, dve_lo[3 + p], lo_dve) if p < 3 else None)
            pooled = pooling(dve, 0, chain)
            normalized = normalize(EMB1, 1)
            for n in range(8):
                if n < 4:
                    next(pooled)
                add_score(2 * n)
                add_score(2 * n + 1)
                if n >= 3:
                    next(normalized)
            select_pair()
            gained = emb_gains(dve, 1, chain)
            for g in pooling(dve, 1, chain):
                if g < 3:
                    next(gained)
            dve.wait_ge(masks01_ready, 2)
            attention(0)
            mix_lo(0, 1)
            add_residual(0, LN1_0)
            x_lo(dve, "x1T", 0, x_lo_dve, (l1_g, l1_b))
            for d in LAST_DOTS:
                add_score(d)
            x1_gains(dve, 0, chain)
            for i in range(CB, NB):
                select(i)
            latent_parts_lo()
            attention(1)
            mix_lo(1, 1)
            add_residual(1, LN1_1)
            split_lo(dve, ("mlp", 1, 0), lo_dve)
            split_lo(dve, ("mlp", 1, 1), lo_dve)
            x_lo(dve, "x1T", 1, x_lo_dve, (l1_g, l1_b))
            with dve.Fori(0, GROUPS - 1) as g:
                mlp_lo(dve, 1, g, False)
            mlp_lo(dve, 1, GROUPS - 1, True, before=first_half)
            last_products()

        @block.scalar
        def _(act):
            def full(name):
                act.wait_ge(g_full, G[name] + 1)

            def copy_out(name, out_ap, in_ap, func=ACT.Copy, **kw):
                full(name)
                nc.scalar.activation(out_ap, in_ap, func, **kw).then_inc(g_evac, 1)

            def transposed(c, what, g, b, sem_lo, lo_before):
                for k in range(KT):
                    name = (what, c, k)
                    full(name)
                    if k >= 2:
                        act.wait_ge(sem_lo, lo_before + k - 1)
                    elif (what, c) in (("xT", 1), ("x1T", 0)):
                        act.wait_ge(iq_lo_ready, 4 if what == "xT" else 8)
                    affine = dict(scale=g[:, k:k + 1], bias=b[:, k:k + 1])
                    if k % 2 == 0 or (what, c) == ("xT", 1):
                        nc.scalar.activation(val[:, k % 2, :], bank(name)[:, :], ACT.Identity, **affine)
                    nc.scalar.activation(xhi[:, k, :], bank(name)[:, :], ACT.Identity, **affine).then_inc(g_evac, 1)

            def hi(name):
                n = U[name]
                act.wait_ge(ring_in[n % 4], arrivals(n))
                if n >= 2:
                    wait_product(act, units[n - 2])
                nc.scalar.activation(parts_of(name, whi[n % 2]), parts_of(name, wring[n % 4]), ACT.Copy).then_inc(hi_ready, 1)

            def hi_after(name):
                hi(units[U[name] + 2])

            def keys_queries(c):
                hi_after(("ik", c))
                ps = bank(("ik", c))
                at = slice(c * CHUNK, (c + 1) * CHUNK)
                full(("ik", c))
                act.wait_ge(x_lo_pool if c else x_lo_dve, KT)
                nc.scalar.activation(val[0:KEYW, 0, :], ps[0:KEYW, :], ACT.Copy)
                nc.scalar.activation(key_hi[0:HD, at], ps[0:HD, :], ACT.Copy)
                nc.scalar.activation(key_hi[HD:P, at], ps[0:HD, :], ACT.Copy).then_inc(g_evac, 1)
                hi_after(("c", c))
                copy_out(("c", c), val[:, 1, :], bank(("c", c))[:, :])
                if c == 0:
                    copy_out("wuk", wukT[:, :, :], bank("wuk")[:, :].rearrange("p (k c) -> p k c", k=4))
                    copy_out("bias", bias_row[:, :], bank("bias")[0:HEADS, 0:FWIN])
                    act.wait_ge(g_evac, EV["bias"])
                    act.sem_inc(bias_row_ready, 1)
                for p in range(4):
                    name = ("iq", c, p)
                    hi_after(name)
                    full(name)
                    if p == 0:
                        act.wait_ge(key_lo_ready, c + 1)
                        full(("iw", c))
                    if p >= 2:
                        act.wait_ge(iq_lo_ready, 4 * c + p - 1)
                    ps = bank(name)
                    nc.scalar.activation(val[:, p % 2, :], ps[:, :], ACT.Copy, scale=HD ** -0.5)
                    nc.scalar.activation(iq2[0:HD, 2 * p, :], ps[0:HD, :], ACT.Copy, scale=HD ** -0.5)
                    nc.scalar.activation(iq2[HD:P, 2 * p + 1, :], ps[HD:P, :], ACT.Copy, scale=HD ** -0.5).then_inc(g_evac, 1)
                    if p == 0:
                        copy_out(("iw", c), idx_w[:, CB * c:CB * c + CB, :],
                                 bank(("iw", c))[:, 0:CB * HEADS].rearrange("p (b h) -> p b h", b=CB), scale=HEADS ** -0.5)
                        copy_out(("cR", c), craw[:, :, :], bank(("cR", c))[:, :].rearrange("p (b n) -> p b n", b=CB))
                        act.wait_ge(g_evac, EV[("cR", c)])
                        if c:
                            act.wait_ge(lat_lo_ready, 1)
                        for b in range(CB):
                            nc.scalar.activation(squares[:, b, :], craw[:, b, :], ACT.Square,
                                                 accum_out=csum[:, CB * c + b:CB * c + b + 1]).then_inc(csum_ready, 1)
                    if p == 2:
                        act.wait_ge(crstd_ready, c + 1)
                        act.wait_ge(csum_ready, CB * c + CB)
                        for b in range(CB):
                            at_b = crstd[:, CB * c + b:CB * c + b + 1]
                            nc.scalar.activation(lat_val[:, b, :], craw[:, b, :], ACT.Copy, scale=at_b)
                            nc.scalar.activation(lat_hi[:, CB * c + b, :], craw[:, b, :], ACT.Copy, scale=at_b)\
                                .then_inc(lat_ready, 1)
                copy_out(("cT", c), latT[:, c * CHUNK:(c + 1) * CHUNK], bank(("cT", c))[:, :], scale=kv_g)

            def relu_dots(n):
                i = n // HEADS + 2
                act.wait_ge(dots_full, n + 1)
                if n >= 2:
                    act.wait_ge(score_added, n - 1)
                nc.scalar.activation(relu_sb[:, n % 2, 0:(i + 1) * P], wide[n % 2][:, 0:(i + 1) * P], ACT.Relu)\
                    .then_inc(relu_ready, 1)

            def products(c):
                unit = 0
                for name in tokens_queries(c):
                    n = name[2]
                    if name[0] == "po":
                        copy_out(name, pool_out[c][:, n, :], bank(name)[:, :], scale=pscale[:, n:n + 1])
                        continue
                    hi_after(name)
                    if name[0] == "q":
                        copy_out(name, qT[:, n, :], bank(name)[:, :])
                    else:
                        if n >= 2:
                            act.wait_ge(pooled_ready, 4 * c + n - 1)
                        copy_out(name, uT[:, n % 2, HIST:HIST + CHUNK], bank(name)[:, :])
                    if c == 0:
                        relu_dots(2 * unit)
                        relu_dots(2 * unit + 1)
                    unit += 1

            def latent_queries(c):
                for h in range(HEADS):
                    copy_out(("ql", c, h), (qlat_hi if c else qlatT)[:, h, :], bank(("ql", c, h))[:, :], scale=HD ** -0.5)

            def exps(m):
                i, h = divmod(m, HEADS)
                act.wait_ge(neg_max_ready, m + 1)
                p = logit[:, m % 2, 0:(i + 1) * P]
                nc.scalar.activation(p, p, ACT.Exp, bias=neg_max[:, m % 2:m % 2 + 1],
                                     accum_out=exp_sum[:, i % 2, h:h + 1]).then_inc(exp_ready, 1)

            def attention(c):
                lo, hi = 32 * c, 32 * c + 32
                exps(lo)
                for step in range(lo, lo + LAST_STEP):
                    if step + 1 < hi:
                        exps(step + 1)
                    for name in attention_step(c, step):
                        ps = bank(name)
                        if name[0] == "tr":
                            m, t = name[1], name[2]
                            i = m // HEADS
                            n = min(4, i + 1 - 4 * t)
                            if m % 2 == 0 and m >= 4:
                                act.wait_ge(g_full, G[("pv", m // 2 - 2)] + 1)
                            copy_out(name, pair_slot(probs_hi, m // 2)[:, 4 * t:4 * t + n, m % 2, :],
                                     ps[:, 0:n * P].rearrange("p (k q) -> p k q", k=n))
                        elif name[0] == "pv":
                            copy_out(name, oT[:, :, :], ps[:, 0:2 * P].rearrange("p (h q) -> p h q", h=2), scale=kv_g)
                        elif name[0] == "uv":
                            i, pair = divmod(name[1], 4)
                            copy_out(name, att[:, i % 2, pair * P:pair * P + P], ps[:, 0:P])
                        else:
                            i = name[1]
                            copy_out(name, att_outT[:, :, i % CB * P:i % CB * P + P],
                                     ps[:, :].rearrange("p (k q) -> p k q", k=4))
                    if step == hi:
                        mix_hi(c, 0)

            def mix_hi(c, n):
                raw, part = ((pool_out[c], pool_hi), (att_outT, att_hi))[n]
                act.wait_ge(masked, 32 * c + 32)
                act.wait_ge(g_evac, EV[("aT", CB * c + CB - 1) if n else ("tr", 32 * c + 31, c)])
                for k in range(4):
                    nc.scalar.activation(part[:, k, :], raw[:, k, :], ACT.Copy).then_inc(mix_hi_ready, 1)

            def normalized(c, l):
                for b in range(CB):
                    n = 4 * l + b
                    act.wait_ge(shift_ready, CB * c + b + 1)
                    nc.scalar.activation(rows[:, b, :], rows[:, b, :], ACT.Identity, scale=rstd[:, n:n + 1],
                                         bias=shift[:, n:n + 1]).then_inc(x1_hat_ready, 1)
                    if c == 0 and b < 2:
                        relu_dots(LAST_DOTS[b])

            def output_projection(c, l):
                mix_hi(c, 1)
                for nh, u, b in projection_steps():
                    if b == CB - 1 and (nh, u) < (1, 2):
                        hi_after(("wo", c, nh, u))
                    for d in dots_after(c, nh, u, b):
                        relu_dots(d)
                normalized(c, l)
                hi(("mlp", c, 0))
                hi(("mlp", c, 1))

            def mlp(c, g, last):
                base, evacs, first = G[("mlp", c, 0)], EV[("mlp", c, 0)], U[("mlp", c, 0)]
                for j in range(GUNITS):
                    nh, u = divmod(j - GT, 4)
                    if j >= GT and u == 3 and not (c == 1 and last):
                        for b in range(CB):
                            n = 8 * GROUPS * c + 4 * nh + b
                            act.wait_ge(wide_full, g * 8 + (n + 1))
                            act.wait_ge(y_added, g * 8 + (n + 1))
                            nc.scalar.activation(y_stage[:, b, :], wide[b // 2][:, (b % 2) * 512:(b % 2) * 512 + 512],
                                                 ACT.Copy).then_inc(y_evac, 1)
                    if last and c == 1 and j >= GUNITS - 2:
                        continue
                    wait_unit_done(act, c, g, j)
                    if not (last and j >= GUNITS - 2):
                        act.wait_ge(ring_in[(first + j + 2) % 4], g * (16 * GUNITS // 4) + arrivals(first + j + 2))
                        nc.scalar.activation(whi[(first + j) % 2][:, :], wring[(first + j + 2) % 4][:, :], ACT.Copy)\
                            .then_inc(hi_ready, 1)
                    else:
                        hi(("wo", 1, 0, j - GUNITS + 2))
                    if j < GT:
                        act.wait_ge(h_lo_ready[c], g * GT + (j + 1))
                        nc.scalar.activation(relu_h[:, j % 2, :], g_bank[(base + j) % 4][:, :], ACT.Relu).then_inc(g_evac, 1)
                        act.wait_ge(g_evac, g * GT + (evacs + j))
                        nc.scalar.activation(hhi[:, j, :], relu_h[:, j % 2, :], ACT.Square)
                        nc.scalar.activation(h_val[:, j % 2, :], relu_h[:, j % 2, :], ACT.Square).then_inc(h_ready, 1)

            def mlp_groups(c):
                act.wait_ge(score_added, 48)
                with act.Fori(0, GROUPS - 1) as g:
                    mlp(c, g, False)
                mlp(c, GROUPS - 1, True)

            act.sem_inc(y_evac, CB)
            copy_out("vecs", vecs[:, :], bank("vecs")[:, 0:37])
            act.wait_ge(g_evac, EV["vecs"])
            hi(units[0])
            transposed(0, "xT", emb_g, emb_b, x_lo_dve, 0)
            hi(units[1])
            keys_queries(0)
            products(0)
            for n in range(4):
                copy_out(("near", n), near_bias[:, 2 * n:2 * n + 2, :],
                         bank(("near", n))[:, :].rearrange("p (h n) -> p h n", h=2))
            act.wait_ge(score_added, 16)
            latent_queries(0)
            transposed(1, "xT", emb_g, emb_b, x_lo_pool, 0)
            keys_queries(1)
            products(1)
            attention(0)
            output_projection(0, LN1_0)
            transposed(0, "x1T", l1_g, l1_b, x_lo_dve, KT)
            act.wait_ge(x_lo_dve, 2 * KT)
            nc.scalar.activation(latT_hi[:, :], latT[:, :], ACT.Copy).then_inc(latT_hi_ready, 1)
            mlp_groups(0)
            latent_queries(1)
            act.wait_ge(y_added, CB + 8 * GROUPS)
            attention(1)
            output_projection(1, LN1_1)
            act.wait_ge(logits_full, 64)
            transposed(1, "x1T", l1_g, l1_b, x_lo_dve, 2 * KT)
            mlp_groups(1)
            for b, at in OUT_SHARED.items():
                act.wait_ge(shift_ready, NB + b + 1)
                n = 4 * LN2_1 + b
                nc.scalar.activation(rows[:, b, at], rows[:, b, at], ACT.Identity, scale=rstd[:, n:n + 1],
                                     bias=shift[:, n:n + 1]).then_inc(last_hat_ready, 1)

        @block.tensor
        def _(pe):
            def free(name):
                if G[name] >= 4:
                    before = uses[G[name] - 4]
                    if before[0] == "proj":
                        pe.wait_ge(wo_added, 8 * before[1] + 4 * before[2] + before[3] + 1)
                    else:
                        pe.wait_ge(g_evac, EV[before])
                    if before[0] in ("xT", "x1T") and before[2] % 2 and before[:2] != ("xT", 1):
                        x_ready(*before)
                    if before[0] == "tr":
                        pe.wait_ge(probs_lo_ready, TR[before])
                    if before[:2] == ("ql", 1):
                        pe.wait_ge(qlat_lo_ready, before[2] + 1)

            def transposes(name, parts):
                free(name)
                ps = bank(name)
                for n, part in enumerate(parts):
                    rows_in_part = part.shape[0]
                    last = nc.tensor.transpose(ps[:, n * P:n * P + rows_in_part] if rows_in_part == P
                                               else ps[:, 0:rows_in_part], part,
                                               ident[0:rows_in_part, 0:rows_in_part])
                last.then_inc(g_full, 1)

            def evacuated(name):
                pe.wait_ge(g_evac, EV[name])

            def x_transposes(c, what):
                if what == "xT":
                    pe.wait_ge(xhat_ready, CB * c + CB)
                else:
                    pe.wait_ge(x1_hat_ready, CB * c + CB)
                for k in range(KT):
                    transposes((what, c, k), [rows[:, b, k * P:(k + 1) * P] for b in range(CB)])

            def x_ready(what, c, k):
                if (what, c) == ("xT", 1):
                    pe.wait_ge(x_lo_pool, k + 1)
                else:
                    pe.wait_ge(x_lo_dve, KT * (0 if what == "xT" else 1 + c) + k + 1)

            def three_passes(out_ap, w_hi, w_lo, m_hi, m_lo, first, last):
                nc.tensor.matmul(out_ap, w_hi, m_hi, start=first, stop=False)
                nc.tensor.matmul(out_ap, w_hi, m_lo, start=False, stop=False)
                return nc.tensor.matmul(out_ap, w_lo, m_hi, start=False, stop=last)

            def column_products(out_ap, slot, x_parts=None):
                h, l = k_columns(whi[slot]), k_columns(wlo[slot])
                m = out_ap.shape[0]
                for k in range(KT):
                    if x_parts:
                        x_ready(*x_parts, k)
                    ins = three_passes(out_ap, h[:, k, 0:m], l[:, k, 0:m], xhi[:, k, :], xlo[:, k, :], k == 0, k == KT - 1)
                return ins

            def project(name, x_parts=None):
                pe.wait_ge(*LO[name])
                free(name)
                m = KEYW if name[0] == "ik" else P
                column_products(bank(name)[0:m, :], U[name] % 2, x_parts).then_inc(g_full, 1)

            def keys_queries(c):
                project(("ik", c), ("xT", c))
                project(("c", c))
                if c == 0:
                    pe.wait_ge(late_in, 16 * 5)
                    transposes("wuk", [wuk_raw[:, k * P:(k + 1) * P] for k in range(4)])
                    free("bias")
                    nc.tensor.matmul(bank("bias")[0:HEADS, 0:FWIN], relb[:, :], hots[:, :], start=True, stop=True).then_inc(g_full, 1)
                project(("iq", c, 0))
                free(("iw", c))
                evacuated(("ik", c))
                for b in range(CB):
                    last = nc.tensor.transpose(bank(("iw", c))[:, b * HEADS:(b + 1) * HEADS], val[HD:KEYW, 0, b * P:(b + 1) * P],
                                               ident[HD:KEYW, HD:KEYW])
                last.then_inc(g_full, 1)
                evacuated(("c", c))
                transposes(("cR", c), [val[:, 1, b * P:(b + 1) * P] for b in range(CB)])
                for p in (1, 2, 3):
                    project(("iq", c, p))
                latent_transposes(c)

            def latent_transposes(c):
                pe.wait_ge(lat_ready, CB * (c + 1))
                transposes(("cT", c), [lat_val[:, b, :] for b in range(CB)])

            def dot(n):
                i, h = n // HEADS + 2, n % HEADS
                if n in (0, 16):
                    pe.wait_ge(key_lo_ready, n // 16 + 1)
                    pe.wait_ge(iq_lo_ready, 4 * (n // 16) + 4)
                if n >= 2:
                    pe.wait_ge(relu_ready, n - 1)
                length = (i + 1) * P
                q = iq2[:, h, i % CB * P:i % CB * P + P]
                for k0 in range(0, length, 512):
                    k1 = max(min(length, k0 + 512), k0 + 256)
                    nc.tensor.matmul(wide[n % 2][:, k0:k1], q, key_hi[:, k0:k1], start=True, stop=False)
                    last = nc.tensor.matmul(wide[n % 2][:, k0:k1], q, key_lo[:, k0:k1], start=False, stop=True)
                last.then_inc(dots_full, 1)

            def latent_queries(c):
                evacuated(("q", c, 3))
                for h in range(HEADS):
                    name = ("ql", c, h)
                    free(name)
                    half = slice((h % 2) * HD, (h % 2) * HD + HD)
                    nc.tensor.matmul(bank(name)[:, :], wukT[half, h // 2, :], qT[half, h // 2, :],
                                     start=True, stop=True).then_inc(g_full, 1)

            def products(c):
                unit = 0
                for name in tokens_queries(c):
                    if name[0] == "po":
                        g = name[2]
                        pe.wait_ge(pooled_ready, 4 * c + g + 1)
                        free(name)
                        nc.tensor.matmul(bank(name)[:, :], poolw[:, g, :], pooledT[:, g % 2, :],
                                         start=True, stop=True).then_inc(g_full, 1)
                        continue
                    project(name)
                    if c == 0:
                        dot(2 * unit)
                        dot(2 * unit + 1)
                    unit += 1

            def logits(m):
                i, h = divmod(m, HEADS)
                length = (i + 1) * P
                if m >= 2:
                    pe.wait_ge(masked, m - 1)
                at = slice(i % CB * P, i % CB * P + P)
                for k0 in range(0, length, 512):
                    k1 = min(length, k0 + 512)
                    if i < CB:
                        last = nc.tensor.matmul(wide[m % 2][:, k0:k1], qlatT[:, h, at], latT[:, k0:k1], start=True, stop=True)
                    else:
                        k1 = max(k1, k0 + 256)
                        last = three_passes(wide[m % 2][:, k0:k1], qlat_hi[:, h, at], qlat_lo[:, h, at],
                                            latT_hi[:, k0:k1], latT_lo[:, k0:k1], True, True)
                last.then_inc(logits_full, 1)

            def attention(c):
                lo, hi = 32 * c, 32 * c + 32
                evacuated(("ql", c, 7))
                pe.wait_ge(relu_ready, 16 if c == 0 else 48)
                if c:
                    pe.wait_ge(latT_lo_ready, 1)
                    pe.wait_ge(qlat_lo_ready, HEADS)
                logits(lo)
                logits(lo + 1)
                for step in range(lo, lo + LAST_STEP):
                    if step + 2 < hi:
                        logits(step + 2)
                    for name in attention_step(c, step):
                        if name[0] == "tr":
                            m, t = name[1], name[2]
                            i = m // HEADS
                            pe.wait_ge(exp_ready, m + 1)
                            transposes(name, [logit[:, m % 2, k * P:(k + 1) * P] for k in range(4 * t, min(4 * t + 4, i + 1))])
                        elif name[0] == "pv":
                            v = name[1]
                            i = v // 4
                            m = 2 * v + 1
                            pe.wait_ge(probs_lo_ready, TR[("tr", m, (i + 4) // 4 - 1)])
                            free(name)
                            for k in range(i + 1):
                                last = three_passes(bank(name)[:, 0:2 * P], lat_hi[:, k, :], lat_lo[:, k, :],
                                                    pair_slot(probs_hi, v)[:, k, :, :].rearrange("p h q -> p (h q)"),
                                                    pair_slot(probs_lo, v)[:, k, :, :].rearrange("p h q -> p (h q)"),
                                                    k == 0, k == i)
                            last.then_inc(g_full, 1)
                        elif name[0] == "uv":
                            v = name[1]
                            evacuated(("pv", v))
                            free(name)
                            for e in range(2):
                                h = 2 * (v % 4) + e
                                last = nc.tensor.matmul(bank(name)[:, e * HD:e * HD + HD], oT[:, e, :],
                                                        wuv[:, h * HD:h * HD + HD], start=True, stop=True)
                            last.then_inc(g_full, 1)
                        else:
                            i = name[1]
                            pe.wait_ge(att_ready, i + 1)
                            transposes(name, [att[:, i % 2, k * P:(k + 1) * P] for k in range(4)])

            def output_projection(c):
                pe.wait_ge(masked, 32 * c + 32)
                for nh in range(2):
                    for u in range(4):
                        name = ("wo", c, nh, u)
                        pe.wait_ge(*LO[name])
                        slot = U[name] % 2
                        h, l = k_pairs(whi[slot]), k_pairs(wlo[slot])
                        m_hi, m_lo = (pool_hi, pool_lo_part) if u < 2 else (att_hi, att_lo)
                        for b in range(CB):
                            acc = bank(("proj", c, nh, b))[:, :]
                            at = slice(b * P, b * P + P)
                            if u == 0:
                                free(("proj", c, nh, b))
                            for k in range(2):
                                f = 2 * (u % 2) + k
                                if nh == 0 and b == 0:
                                    pe.wait_ge(mix_lo_ready, 8 * c + 2 * u + k + 1)
                                last = three_passes(acc, m_hi[:, f, at], m_lo[:, f, at], h[:, k, :], l[:, k, :],
                                                    u == 0 and k == 0, u == 3 and k == 1)
                            if u == 3:
                                last.then_inc(g_full, 1)
                            elif b == CB - 1:
                                last.then_inc(wo_used, 1)
                            for d in dots_after(c, nh, u, b):
                                dot(d)

            def mlp(c):
                base, evacs = G[("mlp", c, 0)], EV[("mlp", c, 0)]
                sem_lo, lo_base = LO[("mlp", c, 0)]
                split = U[("mlp", c, 0)]
                pe.wait_ge(relu_ready, 48)
                pe.wait_ge(masked, 32 * c + 32)
                with pe.Fori(0, GROUPS) as g:
                    for j in range(GUNITS):
                        pe.wait_ge(sem_lo, g * GUNITS + (lo_base + j))
                        slot = (split + j) % 2
                        if j < GT:
                            pe.wait_ge(g_evac, g * GT + (evacs + j - 4))
                            column_products(g_bank[(base + j) % 4][:, :], slot, ("x1T", c) if j == 0 else None)\
                                .then_inc(g_full, 1)
                            continue
                        nh, u = divmod(j - GT, 4)
                        if nh == 0:
                            pe.wait_ge(h_lo_ready[c], g * GT + (2 * u + 2 + 2))
                        h, l = k_pairs(whi[slot]), k_pairs(wlo[slot])
                        for b in range(CB):
                            if u == 0:
                                pe.wait_ge(y_evac, g * 8 + (8 * GROUPS * c + 4 * nh + b + 1))
                            acc = wide[b // 2][:, (b % 2) * 512:(b % 2) * 512 + 512]
                            at = slice(b * P, b * P + P)
                            for k in range(2):
                                f = 2 * u + k
                                last = three_passes(acc, hhi[:, f, at], hlo[:, f, at], h[:, k, :], l[:, k, :],
                                                    f == 0, f == GT - 1)
                            if u == 3:
                                last.then_inc(wide_full, 1)
                        if u < 3:
                            last.then_inc(unit_used, 1)

            pe.wait_ge(ident_ready, 2)
            pe.wait_ge(small_in, 16 * 6)
            transposes("vecs", [vec_rows[:, :]])
            x_transposes(0, "xT")
            keys_queries(0)
            products(0)
            pe.wait_ge(bias_in, 16)
            for n in range(4):
                free(("near", n))
                nc.tensor.matmul(bank(("near", n))[:, :], flip[:, :], near_up[:, 2 * n:2 * n + 2, :].rearrange("p h n -> p (h n)"),
                                 start=True, stop=True).then_inc(g_full, 1)
            latent_queries(0)
            x_transposes(1, "xT")
            keys_queries(1)
            products(1)
            attention(0)
            output_projection(0)
            for d in LAST_DOTS:
                dot(d)
            x_transposes(0, "x1T")
            mlp(0)
            latent_queries(1)
            attention(1)
            output_projection(1)
            x_transposes(1, "x1T")
            mlp(1)


_INS = ["x", "emb_ln_g", "emb_ln_b", "rel_bias", "w_in", "pool_w", "pool_scale", "kv_norm_g", "w_uk", "w_uv", "w_o",
        "ln1_g", "ln1_b", "w_up", "w_down", "ln2_g", "ln2_b"]


def kernel(**inputs):
    import concourse.bacc as bacc
    from concourse.bass_utils import run_bass_kernel_spmd

    nc = bacc.Bacc("TRN2", target_bir_lowering=False, num_devices=1, dynamic_dma_scratch_size=1024)
    arrays, args = {}, []
    for name in _INS:
        a = np.ascontiguousarray(inputs[name])
        arrays[f"in_{name}"] = a
        args.append(nc.dram_tensor(f"in_{name}", a.shape, mybir.dt.from_np(a.dtype), kind="ExternalInput").ap())
    arrays["in_buckets"] = bucket_differences()
    args.append(nc.dram_tensor("in_buckets", (NBUCKET, FWIN), F32, kind="ExternalInput").ap())
    args.append(nc.dram_tensor("normalized_rows", (S, D), F32).ap())
    args.append(nc.dram_tensor("bias_rows", (HEADS, FWIN), F32).ap())
    args.append(nc.dram_tensor("out_0", (1, S, D), F32, kind="ExternalOutput").ap())
    layer(nc, *args)
    r = run_bass_kernel_spmd(nc, [arrays], core_ids=[0])
    return r.results[0]["out_0"]
```
